# Optimizing a Trainium2 kernel written in Bass

```python
import math
import jax, jax.numpy as jnp
from jax import lax
import numpy as np

D_MODEL = 1024
BATCH = 1
SEQ = 512
DEPTH = 1

GRID_W = 64
CTX_LEN = 256
N_MIXERS = 2
N_CONV_LAYERS = (DEPTH + N_MIXERS - 1) // N_MIXERS
N_DELTA_LAYERS = DEPTH // N_MIXERS
CONV_WIDTH = 31
DN_HEADS = 8
DN_HEAD_DIM = D_MODEL // DN_HEADS
DN_SHORT_CONV = 5
DN_CHUNK = 64
N_DIRS = 2
DN_QKV = 3 * D_MODEL
DN_IN = 4 * D_MODEL + 2 * N_DIRS * DN_HEADS
FFN_HIDDEN = 4 * D_MODEL
EPS = 1e-6


def rms_norm(x, g):
    xf = x.astype(jnp.float32)
    y = xf * lax.rsqrt(jnp.mean(xf * xf, axis=-1, keepdims=True) + EPS)
    return (y * g.astype(jnp.float32)).astype(x.dtype)

def layer_norm(x, g, b):
    xf = x.astype(jnp.float32)
    mu = jnp.mean(xf, axis=-1, keepdims=True)
    xc = xf - mu
    y = xc * lax.rsqrt(jnp.mean(xc * xc, axis=-1, keepdims=True) + EPS)
    return (y * g.astype(jnp.float32) + b.astype(jnp.float32)).astype(x.dtype)

def l2_norm(x):
    xf = x.astype(jnp.float32)
    return xf * lax.rsqrt(jnp.sum(xf * xf, axis=-1, keepdims=True) + EPS)

def modulate(h, shift, scale):
    return h * (1.0 + scale) + shift

def dwconv(x, w):
    K, C = w.shape
    return lax.conv_general_dilated(
        x, w[:, None, :].astype(x.dtype), window_strides=(1,),
        padding=[(K // 2, K // 2)], dimension_numbers=('NWC', 'WIO', 'NWC'),
        feature_group_count=C)

def conformer_conv(h, n_seg, w_pw1, b_pw1, w_dw, b_dw, ln_g, ln_b, w_pw2, b_pw2):
    B, L, D = h.shape
    u = h @ w_pw1 + b_pw1
    a, gate = jnp.split(u, 2, axis=-1)
    u = a * jax.nn.sigmoid(gate)
    u = dwconv(u.reshape(B * n_seg, L // n_seg, D), w_dw).reshape(B, L, D) + b_dw
    u = jax.nn.silu(layer_norm(u, ln_g, ln_b))
    return u @ w_pw2 + b_pw2

def gated_delta_chunked(q, k, v, g, beta, state):
    B, H, L, DK = q.shape
    DV = v.shape[-1]
    C = DN_CHUNK
    NC = L // C
    q = q.reshape(B, H, NC, C, DK)
    k = k.reshape(B, H, NC, C, DK)
    v = v.reshape(B, H, NC, C, DV)
    g = g.reshape(B, H, NC, C)
    beta = beta.reshape(B, H, NC, C)
    G = jnp.cumsum(g, axis=-1)
    lower = jnp.tril(jnp.ones((C, C), dtype=bool))
    strict = jnp.tril(jnp.ones((C, C), dtype=bool), -1)
    decay = jnp.exp(jnp.where(lower, G[..., :, None] - G[..., None, :], -jnp.inf))
    kk = jnp.einsum('bhncd,bhnsd->bhncs', k, k)
    a_mat = jnp.where(strict, beta[..., :, None] * kk * decay, 0.0)
    eye = jnp.broadcast_to(jnp.eye(C, dtype=q.dtype), a_mat.shape)
    rhs = jnp.concatenate([beta[..., None] * v, (beta * jnp.exp(G))[..., None] * k], axis=-1)
    sol = lax.linalg.triangular_solve(a_mat + eye, rhs, left_side=True, lower=True,
                                      unit_diagonal=True)
    u, w = sol[..., :DV], sol[..., DV:]
    qk = jnp.einsum('bhncd,bhnsd->bhncs', q, k) * decay
    qg = q * jnp.exp(G)[..., None]
    kd = k * jnp.exp(G[..., -1:] - G)[..., None]
    chunk_decay = jnp.exp(G[..., -1])
    xs = tuple(jnp.moveaxis(t, 2, 0) for t in (u, w, qg, qk, kd, chunk_decay))

    def step(S, inp):
        u_c, w_c, qg_c, qk_c, kd_c, cd_c = inp
        v_new = u_c - jnp.einsum('bhcd,bhde->bhce', w_c, S)
        o_c = (jnp.einsum('bhcd,bhde->bhce', qg_c, S)
               + jnp.einsum('bhcs,bhse->bhce', qk_c, v_new))
        S = S * cd_c[..., None, None] + jnp.einsum('bhcd,bhce->bhde', kd_c, v_new)
        return S, o_c

    state, o = lax.scan(step, state, xs)
    o = jnp.moveaxis(o, 0, 2).reshape(B, H, L, DV)
    return o, state

def gdn_project(h, w_in, conv_w, a_log, dt_bias):
    B, L, _ = h.shape
    p = h @ w_in
    qkv = jax.nn.silu(dwconv(p[..., :DN_QKV], conv_w))
    z = p[..., DN_QKV:4 * D_MODEL].reshape(B, L, DN_HEADS, DN_HEAD_DIM)
    ab = p[..., 4 * D_MODEL:].astype(jnp.float32).reshape(B, L, 2, N_DIRS, DN_HEADS)
    to_heads = lambda t: t.reshape(B, L, DN_HEADS, DN_HEAD_DIM).transpose(0, 2, 1, 3)
    q, k, v = jnp.split(qkv, 3, axis=-1)
    q = l2_norm(to_heads(q)) * (DN_HEAD_DIM ** -0.5)
    k = l2_norm(to_heads(k))
    v = to_heads(v).astype(jnp.float32)
    g = -jnp.exp(a_log.astype(jnp.float32)) * jax.nn.softplus(ab[:, :, 0] + dt_bias.astype(jnp.float32))
    beta = jax.nn.sigmoid(ab[:, :, 1])
    return q, k, v, z, jnp.transpose(g, (2, 0, 3, 1)), jnp.transpose(beta, (2, 0, 3, 1))

def gdn_output(o, z, norm_g, w_o, dtype):
    B, H, L, DV = o.shape
    o = rms_norm(o.transpose(0, 2, 1, 3), norm_g) * jax.nn.silu(z.astype(jnp.float32))
    return o.reshape(B, L, H * DV).astype(dtype) @ w_o

def gated_deltanet_bidir(hc, hl, w_in, conv_w, a_log, dt_bias, norm_g, w_o):
    qc, kc, vc, zc, gc, bc = gdn_project(hc, w_in, conv_w, a_log, dt_bias)
    ql, kl, vl, zl, gl, bl = gdn_project(hl, w_in, conv_w, a_log, dt_bias)
    B = hl.shape[0]
    s0 = jnp.zeros((B, DN_HEADS, DN_HEAD_DIM, DN_HEAD_DIM), jnp.float32)
    fl = lambda t: jnp.flip(t, axis=2)
    oc_f, sc_f = gated_delta_chunked(qc, kc, vc, gc[0], bc[0], s0)
    ol_f, _ = gated_delta_chunked(ql, kl, vl, gl[0], bl[0], sc_f)
    oc_b, sc_b = gated_delta_chunked(fl(qc), fl(kc), fl(vc), fl(gc[1]), fl(bc[1]), s0)
    ol_b, _ = gated_delta_chunked(fl(ql), fl(kl), fl(vl), fl(gl[1]), fl(bl[1]), sc_b)
    yc = gdn_output(oc_f + fl(oc_b), zc, norm_g, w_o, hc.dtype)
    yl = gdn_output(ol_f + fl(ol_b), zl, norm_g, w_o, hl.dtype)
    return yc, yl

def sq_relu_mlp(h, w1, w2):
    return jnp.square(jax.nn.relu(h @ w1)) @ w2

def first_inputs(seed: int = 0) -> dict:
    key = jax.random.key(seed)
    ks = jax.random.split(key, 26)
    D = D_MODEL
    NA, NB = N_CONV_LAYERS, N_DELTA_LAYERS
    nrm = lambda k, shape, s: jax.random.normal(k, shape, jnp.float32) * s
    dt = jnp.exp(jax.random.uniform(ks[20], (NB, N_DIRS, DN_HEADS), jnp.float32,
                                    minval=math.log(1e-3), maxval=math.log(1e-1)))
    return {
        "x": nrm(ks[0], (BATCH, SEQ, D), 1.0),
        "c": nrm(ks[1], (BATCH, D), 1.0),
        "ctx": nrm(ks[2], (BATCH, CTX_LEN, D), 1.0),
        "c_ctx": nrm(ks[3], (D,), 1.0),
        "w_mod": nrm(ks[4], (DEPTH, D, 6 * D), 0.5 * D ** -0.5),
        "b_mod": nrm(ks[5], (DEPTH, 6 * D), 0.02),
        "norm1_g": 1.0 + nrm(ks[6], (DEPTH, D), 0.02),
        "norm2_g": 1.0 + nrm(ks[7], (DEPTH, D), 0.02),
        "final_g": 1.0 + nrm(ks[8], (D,), 0.02),
        "conv_w_pw1": nrm(ks[9], (NA, D, 2 * D), D ** -0.5),
        "conv_b_pw1": nrm(ks[10], (NA, 2 * D), 0.02),
        "conv_w_dw": nrm(ks[11], (NA, CONV_WIDTH, D), CONV_WIDTH ** -0.5),
        "conv_b_dw": nrm(ks[12], (NA, D), 0.02),
        "conv_ln_g": 1.0 + nrm(ks[13], (NA, D), 0.02),
        "conv_ln_b": nrm(ks[14], (NA, D), 0.02),
        "conv_w_pw2": nrm(ks[15], (NA, D, D), D ** -0.5),
        "conv_b_pw2": nrm(ks[16], (NA, D), 0.02),
        "dn_w_in": nrm(ks[17], (NB, D, DN_IN), D ** -0.5),
        "dn_conv_w": nrm(ks[18], (NB, DN_SHORT_CONV, DN_QKV), DN_SHORT_CONV ** -0.5),
        "dn_a_log": jnp.log(jax.random.uniform(ks[19], (NB, N_DIRS, DN_HEADS), jnp.float32,
                                               minval=1.0, maxval=16.0)),
        "dn_dt_bias": dt + jnp.log(-jnp.expm1(-dt)),
        "dn_norm_g": 1.0 + nrm(ks[21], (NB, DN_HEAD_DIM), 0.02),
        "dn_w_o": nrm(ks[22], (NB, D, D), D ** -0.5),
        "mlp_w1": nrm(ks[23], (DEPTH, D, FFN_HIDDEN), D ** -0.5),
        "mlp_w2": nrm(ks[24], (DEPTH, FFN_HIDDEN, D), FFN_HIDDEN ** -0.5),
    }

def first_block(x, c, ctx, c_ctx, w_mod, b_mod, norm1_g, norm2_g, final_g,
              conv_w_pw1, conv_b_pw1, conv_w_dw, conv_b_dw, conv_ln_g, conv_ln_b,
              conv_w_pw2, conv_b_pw2, dn_w_in, dn_conv_w, dn_a_log, dn_dt_bias,
              dn_norm_g, dn_w_o, mlp_w1, mlp_w2):
    rows = x.shape[1] // GRID_W
    xl, xc = x, ctx
    sc_l = jax.nn.silu(c)
    sc_c = jax.nn.silu(c_ctx)
    for i in range(DEPTH):
        last = i == DEPTH - 1
        j = i // N_MIXERS
        mod_l = (sc_l @ w_mod[i] + b_mod[i])[:, None, :]
        mod_c = (sc_c @ w_mod[i] + b_mod[i])[None, None, :]
        sh1_l, s1_l, g1_l, sh2_l, s2_l, g2_l = jnp.split(mod_l, 6, axis=-1)
        sh1_c, s1_c, g1_c, sh2_c, s2_c, g2_c = jnp.split(mod_c, 6, axis=-1)
        hl = modulate(rms_norm(xl, norm1_g[i]), sh1_l, s1_l)
        hc = modulate(rms_norm(xc, norm1_g[i]), sh1_c, s1_c)
        if i % N_MIXERS == 0:
            conv_p = (conv_w_pw1[j], conv_b_pw1[j], conv_w_dw[j], conv_b_dw[j],
                      conv_ln_g[j], conv_ln_b[j], conv_w_pw2[j], conv_b_pw2[j])
            yl = conformer_conv(hl, rows, *conv_p)
            if not last:
                yc = conformer_conv(hc, 1, *conv_p)
        else:
            yc, yl = gated_deltanet_bidir(hc, hl, dn_w_in[j], dn_conv_w[j], dn_a_log[j],
                                          dn_dt_bias[j], dn_norm_g[j], dn_w_o[j])
        xl = xl + g1_l * yl
        xl = xl + g2_l * sq_relu_mlp(modulate(rms_norm(xl, norm2_g[i]), sh2_l, s2_l),
                                     mlp_w1[i], mlp_w2[i])
        if not last:
            xc = xc + g1_c * yc
            xc = xc + g2_c * sq_relu_mlp(modulate(rms_norm(xc, norm2_g[i]), sh2_c, s2_c),
                                         mlp_w1[i], mlp_w2[i])
    return rms_norm(xl, final_g)


DEPTH_2 = 2

N_DIFF_HEADS = 6
DIFF_HEAD_DIM = 64
DIFF_V_DIM = 2 * DIFF_HEAD_DIM
N_FOURIER_GROUPS = 4
FOURIER_GROUP_DIM = 64
ATTN_QK_W = N_DIFF_HEADS * 2 * DIFF_HEAD_DIM
ATTN_V_W = N_DIFF_HEADS * DIFF_V_DIM
FOURIER_W = N_FOURIER_GROUPS * FOURIER_GROUP_DIM
EVEN_IN_W = 2 * ATTN_QK_W + ATTN_V_W + FOURIER_W
EVEN_MIX_W = ATTN_V_W + FOURIER_W
CONV_K = 3
N_EXPERTS = 16
EC_CAPACITY_FACTOR = 2
D_EXPERT = 1024
ROPE_BASE = 10000.0
Q_BLOCK = 128
N_EVEN = (DEPTH_2 + 1) // 2
N_ODD = DEPTH_2 // 2


def rmsnorm(x, g):
    xf = x.astype(jnp.float32)
    y = xf * lax.rsqrt(jnp.mean(xf * xf, axis=-1, keepdims=True) + EPS)
    return (y * g.astype(jnp.float32)).astype(x.dtype)

def modulate_2(x, g, shift, scale):
    return rmsnorm(x, g) * (1 + scale) + shift

def ada_params(cond, w_ada, b_ada):
    m = jax.nn.silu(cond) @ w_ada + b_ada
    return jnp.split(m[..., None, :], 6, axis=-1)

def axial_rope(n, dtype):
    rows = n // GRID_W
    r = jnp.repeat(jnp.arange(rows, dtype=jnp.float32), GRID_W)
    col = jnp.tile(jnp.arange(GRID_W, dtype=jnp.float32), rows)
    n_freq = DIFF_HEAD_DIM // 4
    inv = ROPE_BASE ** (-jnp.arange(n_freq, dtype=jnp.float32) / n_freq)
    ar = r[:, None] * inv
    ac = col[:, None] * inv
    ang = jnp.concatenate([ar, ar, ac, ac], axis=-1)
    return jnp.cos(ang).astype(dtype), jnp.sin(ang).astype(dtype)

def apply_rope(x, cos, sin):
    x1, x2, x3, x4 = jnp.split(x, 4, axis=-1)
    rot = jnp.concatenate([-x2, x1, -x4, x3], axis=-1)
    return x * cos[None, :, None, None, :] + rot * sin[None, :, None, None, :]

def qk_heads(t):
    return t.reshape(t.shape[0], t.shape[1], N_DIFF_HEADS, 2, DIFF_HEAD_DIM)

def v_heads(t):
    return t.reshape(t.shape[0], t.shape[1], N_DIFF_HEADS, DIFF_V_DIM)

def diff_attend(q, k, v, lam):
    s = jnp.einsum('bqhmd,bkhmd->bhmqk', q, k).astype(jnp.float32)
    p = jax.nn.softmax(s, axis=-1)
    a = p[:, :, 0] - lam * p[:, :, 1]
    return jnp.einsum('bhqk,bkhe->bqhe', a.astype(v.dtype), v)

def blocked_diff_attend(q, k, v, lam):
    b, n = q.shape[0], q.shape[1]
    qb = q.reshape(b, n // Q_BLOCK, Q_BLOCK, N_DIFF_HEADS, 2, DIFF_HEAD_DIM).swapaxes(0, 1)
    out = lax.map(lambda qq: diff_attend(qq, k, v, lam), qb)
    return out.swapaxes(0, 1).reshape(b, n, N_DIFF_HEADS, DIFF_V_DIM)

def fourier_mix(f):
    b, n = f.shape[0], f.shape[1]
    fg = f.reshape(b, n, N_FOURIER_GROUPS, FOURIER_GROUP_DIM).astype(jnp.float32)
    y = jnp.fft.fft2(fg, axes=(1, 3), norm='ortho').real
    return y.reshape(b, n, FOURIER_W).astype(f.dtype)

def merge_even(att, f, subln, lam_init, w_out):
    b, n = att.shape[0], att.shape[1]
    att = rmsnorm(att, subln) * (1.0 - lam_init)
    o = jnp.concatenate([att.reshape(b, n, ATTN_V_W), fourier_mix(f)], axis=-1)
    return o @ w_out

def even_mixer(h, hc, w_in, q_norm, k_norm, lam, subln, w_out, lam_init, cos, sin, ctx_out):
    scale = DIFF_HEAD_DIM ** -0.5
    cuts = [ATTN_QK_W, 2 * ATTN_QK_W, 2 * ATTN_QK_W + ATTN_V_W]
    q, k, v, f = jnp.split(h @ w_in, cuts, axis=-1)
    q = apply_rope(rmsnorm(qk_heads(q), q_norm), cos, sin) * scale
    k = apply_rope(rmsnorm(qk_heads(k), k_norm), cos, sin)
    qc = None
    fc = None
    if ctx_out:
        qc, kc, vc, fc = jnp.split(hc @ w_in, cuts, axis=-1)
    else:
        kc, vc = jnp.split(hc @ w_in[:, ATTN_QK_W:2 * ATTN_QK_W + ATTN_V_W], [ATTN_QK_W], axis=-1)
    kc = rmsnorm(qk_heads(kc), k_norm)
    vc = v_heads(vc)
    keys = jnp.concatenate([k, kc], axis=1)
    vals = jnp.concatenate([v_heads(v), vc], axis=1)
    y = merge_even(blocked_diff_attend(q, keys, vals, lam), f, subln, lam_init, w_out)
    yc = None
    if ctx_out:
        qc = rmsnorm(qk_heads(qc), q_norm) * scale
        yc = merge_even(diff_attend(qc, kc, vc, lam), fc, subln, lam_init, w_out)
    return y, yc

def shortconv(z, w):
    zp = jnp.pad(z, ((0, 0), (1, 1), (0, 0)))
    return w[0] * zp[:, :-2] + w[1] * zp[:, 1:-1] + w[2] * zp[:, 2:]

def odd_mixer(h, w_in, conv_w, w_out):
    bg, cg, u = jnp.split(h @ w_in, 3, axis=-1)
    return (bg * shortconv(cg * u, conv_w)) @ w_out

def ec_moe(h, w_router, w_gate, w_up, w_down):
    b, n, d = h.shape
    cap = EC_CAPACITY_FACTOR * n // N_EXPERTS
    aff = jax.nn.softmax(h.astype(jnp.float32) @ w_router.astype(jnp.float32), axis=-1)
    g, idx = lax.top_k(aff.swapaxes(1, 2), cap)
    xs = jax.vmap(lambda hb, ib: hb[ib])(h, idx)
    a = jax.nn.silu(jnp.einsum('becd,edf->becf', xs, w_gate)) * jnp.einsum('becd,edf->becf', xs, w_up)
    y = jnp.einsum('becf,efd->becd', a, w_down) * g[..., None].astype(h.dtype)
    return jax.vmap(lambda yb, ib: jnp.zeros((n, d), yb.dtype).at[ib.reshape(-1)].add(yb.reshape(-1, d)))(y, idx)

def second_inputs(seed: int = 0) -> dict:
    key = jax.random.key(seed)
    ks = jax.random.split(key, 24)

    def nrm(k, shape, s):
        return jax.random.normal(k, shape, jnp.float32) * s

    D = D_MODEL
    return {
        'x': nrm(ks[0], (BATCH, SEQ, D), 1.0),
        'c': nrm(ks[1], (BATCH, D), 1.0),
        'ctx': nrm(ks[2], (BATCH, CTX_LEN, D), 1.0),
        'c_ctx': nrm(ks[3], (D,), 1.0),
        'ada_w': nrm(ks[4], (DEPTH_2, D, 6 * D), 0.5 * D ** -0.5),
        'ada_b': nrm(ks[5], (DEPTH_2, 6 * D), 0.02),
        'norm_mix': 1.0 + nrm(ks[6], (DEPTH_2, D), 0.02),
        'norm_ffn': 1.0 + nrm(ks[7], (DEPTH_2, D), 0.02),
        'attn_w_in': nrm(ks[8], (N_EVEN, D, EVEN_IN_W), D ** -0.5),
        'attn_q_norm': 1.0 + nrm(ks[9], (N_EVEN, DIFF_HEAD_DIM), 0.02),
        'attn_k_norm': 1.0 + nrm(ks[10], (N_EVEN, DIFF_HEAD_DIM), 0.02),
        'lam_q1': nrm(ks[11], (N_EVEN, DIFF_HEAD_DIM), 0.1),
        'lam_k1': nrm(ks[12], (N_EVEN, DIFF_HEAD_DIM), 0.1),
        'lam_q2': nrm(ks[13], (N_EVEN, DIFF_HEAD_DIM), 0.1),
        'lam_k2': nrm(ks[14], (N_EVEN, DIFF_HEAD_DIM), 0.1),
        'attn_subln': 1.0 + nrm(ks[15], (N_EVEN, DIFF_V_DIM), 0.02),
        'attn_w_out': nrm(ks[16], (N_EVEN, EVEN_MIX_W, D), EVEN_MIX_W ** -0.5),
        'conv_w_in': nrm(ks[17], (N_ODD, D, 3 * D), D ** -0.5),
        'conv_w': nrm(ks[18], (N_ODD, CONV_K, D), CONV_K ** -0.5),
        'conv_w_out': nrm(ks[19], (N_ODD, D, D), D ** -0.5),
        'router_w': nrm(ks[20], (DEPTH_2, D, N_EXPERTS), D ** -0.5),
        'moe_w_gate': nrm(ks[21], (DEPTH_2, N_EXPERTS, D, D_EXPERT), D ** -0.5),
        'moe_w_up': nrm(ks[22], (DEPTH_2, N_EXPERTS, D, D_EXPERT), D ** -0.5),
        'moe_w_down': nrm(ks[23], (DEPTH_2, N_EXPERTS, D_EXPERT, D), D_EXPERT ** -0.5),
    }

def second_block(x, c, ctx, c_ctx, ada_w, ada_b, norm_mix, norm_ffn,
              attn_w_in, attn_q_norm, attn_k_norm, lam_q1, lam_k1, lam_q2, lam_k2,
              attn_subln, attn_w_out, conv_w_in, conv_w, conv_w_out,
              router_w, moe_w_gate, moe_w_up, moe_w_down):
    cos, sin = axial_rope(x.shape[1], x.dtype)
    xc = ctx
    for l in range(DEPTH_2):
        ctx_out = any(j % 2 == 0 for j in range(l + 1, DEPTH_2))
        ctx_in = (l % 2 == 0) or ctx_out
        sh_m, sc_m, g_m, sh_f, sc_f, g_f = ada_params(c, ada_w[l], ada_b[l])
        h = modulate_2(x, norm_mix[l], sh_m, sc_m)
        hc = None
        cg_m = cg_f = csh_f = csc_f = None
        if ctx_in:
            csh_m, csc_m, cg_m, csh_f, csc_f, cg_f = ada_params(c_ctx, ada_w[l], ada_b[l])
            hc = modulate_2(xc, norm_mix[l], csh_m, csc_m)
        if l % 2 == 0:
            e = l // 2
            lam_init = 0.8 - 0.6 * math.exp(-0.3 * l)
            lam = (jnp.exp(jnp.sum(lam_q1[e].astype(jnp.float32) * lam_k1[e].astype(jnp.float32)))
                   - jnp.exp(jnp.sum(lam_q2[e].astype(jnp.float32) * lam_k2[e].astype(jnp.float32)))
                   + lam_init)
            y, yc = even_mixer(h, hc, attn_w_in[e], attn_q_norm[e], attn_k_norm[e], lam,
                               attn_subln[e], attn_w_out[e], lam_init, cos, sin, ctx_out)
        else:
            o = l // 2
            y = odd_mixer(h, conv_w_in[o], conv_w[o], conv_w_out[o])
            yc = odd_mixer(hc, conv_w_in[o], conv_w[o], conv_w_out[o]) if ctx_out else None
        x = x + g_m * y
        x = x + g_f * ec_moe(modulate_2(x, norm_ffn[l], sh_f, sc_f),
                             router_w[l], moe_w_gate[l], moe_w_up[l], moe_w_down[l])
        if ctx_out:
            xc = xc + cg_m * yc
            xc = xc + cg_f * ec_moe(modulate_2(xc, norm_ffn[l], csh_f, csc_f),
                                    router_w[l], moe_w_gate[l], moe_w_up[l], moe_w_down[l])
    return x


def setup_inputs(seed=0):
    out = dict(first_inputs(seed))
    for name, value in second_inputs(seed + 1).items():
        if name != "x":
            out[name + "_2"] = value
    return out


def reference(
    x, c, ctx, c_ctx, w_mod, b_mod, norm1_g, norm2_g, final_g, conv_w_pw1, conv_b_pw1,
    conv_w_dw, conv_b_dw, conv_ln_g, conv_ln_b, conv_w_pw2, conv_b_pw2, dn_w_in, dn_conv_w,
    dn_a_log, dn_dt_bias, dn_norm_g, dn_w_o, mlp_w1, mlp_w2, c_2, ctx_2, c_ctx_2, ada_w_2,
    ada_b_2, norm_mix_2, norm_ffn_2, attn_w_in_2, attn_q_norm_2, attn_k_norm_2, lam_q1_2,
    lam_k1_2, lam_q2_2, lam_k2_2, attn_subln_2, attn_w_out_2, conv_w_in_2, conv_w_2,
    conv_w_out_2, router_w_2, moe_w_gate_2, moe_w_up_2, moe_w_down_2,
):
    x = first_block(
        x, c, ctx, c_ctx, w_mod, b_mod, norm1_g, norm2_g, final_g, conv_w_pw1, conv_b_pw1,
        conv_w_dw, conv_b_dw, conv_ln_g, conv_ln_b, conv_w_pw2, conv_b_pw2, dn_w_in, dn_conv_w,
        dn_a_log, dn_dt_bias, dn_norm_g, dn_w_o, mlp_w1, mlp_w2,
    )
    return second_block(
        x, c_2, ctx_2, c_ctx_2, ada_w_2, ada_b_2, norm_mix_2, norm_ffn_2, attn_w_in_2,
        attn_q_norm_2, attn_k_norm_2, lam_q1_2, lam_k1_2, lam_q2_2, lam_k2_2, attn_subln_2,
        attn_w_out_2, conv_w_in_2, conv_w_2, conv_w_out_2, router_w_2, moe_w_gate_2, moe_w_up_2,
        moe_w_down_2,
    )


_drawn_inputs = setup_inputs


def setup_inputs(seed=0):
    import zlib

    import numpy as np

    out = dict(_drawn_inputs(seed))
    spreads = {}
    factors = {'norm1_g': 8.0,
     'norm2_g': 4.751,
     'conv_b_pw1': 8.0,
     'conv_b_dw': 6.403,
     'conv_ln_g': 8.0,
     'conv_ln_b': 8.0,
     'conv_b_pw2': 6.919,
     'norm_mix_2': 4.344,
     'norm_ffn_2': 5.709,
     'attn_q_norm_2': 8.0,
     'attn_k_norm_2': 8.0,
     'lam_q2_2': 3.125,
     'lam_k2_2': 2.686,
     'attn_subln_2': 8.0}
    for name, (base, spread) in spreads.items():
        noise = np.random.default_rng([zlib.crc32(name.encode()), seed]).standard_normal(out[name].shape)
        drawn = base * np.exp(spread * noise) if base else spread * noise
        out[name] = __import__('jax').numpy.asarray(drawn.astype(out[name].dtype))
    for name, factor in factors.items():
        out[name] = (out[name] * factor).astype(out[name].dtype)
    return out
```

```python
from contextlib import ExitStack

import numpy as np

import concourse.bass as bass
from concourse import mybir

F32 = mybir.dt.float32
ALU = mybir.AluOpType
ACT = mybir.ActivationFunctionType
AX = mybir.AxisListType

P = 128
D = 1024
DT = D // P
N = 512
NT = N // P
NC = 256
CT = NC // P
NK = N + NC
SEGS = 8
SEG = 64
TAPS = 31
PAD = TAPS // 2
SEGP = SEG + 2 * PAD
HEADS = 6
HD = 64
QKW = HEADS * 2 * HD
E = 16
CAP = 2 * N // E
PAIRS = E // 2
EPS = 1e-6
N_VEC = 25
LAM_INIT = 0.2
RING = 6
BLK = DT * N

COL = {}
_at = 0
for _n, _w in (
    ("c", 8), ("c2", 8), ("cctx", 8), ("norm1_g", 8), ("norm2_g", 8), ("final_g", 8), ("b_pw1", 16), ("b_dw", 8),
    ("ln_g", 8), ("ln_b", 8), ("b_pw2", 8), ("mix_g", 16), ("ffn_g", 16),
    ("b_mod0", 48), ("b_mod1", 48), ("w_conv3", 24), ("q_g", 1), ("k_g", 1), ("subln", 1), ("unused", 5),
    ("b_mod2", 48), ("w_dw", TAPS * 8),
):
    COL[_n] = _at
    _at += _w
VEC_ROWS = [128, 123, 128, 128, 40]

KCOL = {}
_at = 0
for _n, _w in (("ident", 128), ("ones_d", 128), ("ones_v", 128), ("ones_h", 128), ("rope", 128), ("dft_d", 256),
               ("cos", N), ("sin", N), ("iota", CAP)):
    KCOL[_n] = (_at, _w)
    _at += _w
KW = _at


def constants():
    k = np.zeros((P, KW), np.float32)

    def put(name, a):
        at, w = KCOL[name]
        k[:, at:at + w] = a

    put("ident", np.eye(P))
    put("ones_d", np.full((P, P), 1.0 / D))
    put("ones_v", np.full((P, P), 1.0 / P))
    put("ones_h", np.kron(np.eye(2), np.full((HD, HD), 1.0 / HD)))
    rope = np.zeros((HD, HD))
    for i in range(16):
        rope[16 + i, i] = rope[48 + i, 32 + i] = -1
        rope[i, 16 + i] = rope[32 + i, 48 + i] = 1
    put("rope", np.kron(np.eye(2), rope))
    d = np.arange(HD)
    ang = 2 * np.pi * (np.outer(d, d) % HD) / HD
    put("dft_d", np.hstack([np.kron(np.eye(2), f(ang) / 8.0) for f in (np.cos, np.sin)]))
    inv = (np.float32(10000.0) ** (-np.arange(16, dtype=np.float32) / np.float32(16))).astype(np.float32)
    row, col = np.arange(N) // 64, np.arange(N) % 64
    ar, ac = (np.outer(inv, t.astype(np.float32)).astype(np.float32) for t in (row, col))
    ang = np.vstack([ar, ar, ac, ac] * 2)
    put("cos", np.cos(ang.astype(np.float64)))
    put("sin", np.sin(ang.astype(np.float64)))
    put("iota", np.arange(1, CAP + 1)[None, :])
    t = np.arange(N)
    ang = 2 * np.pi * (np.outer(t, t) % N) / N
    dft_n = (np.vstack([np.cos(ang), -np.sin(ang)]) / np.sqrt(N)).astype(np.float32)
    return k, dft_n


def block_kernel(nc, A, out):
    def blk(w, r0, c0):
        return w[r0:r0 + D, c0:c0 + N].rearrange("(k p) n -> p k n", p=P)

    mods = [A["w_mod"][0], A["ada_w_2"][0], A["ada_w_2"][1]]
    stream = []
    owner_release = []

    tile_by = []

    def tiles(engines):
        t0 = len(tile_by)
        tile_by.extend(engines)
        return t0

    def add(src, release, slot=None):
        n = len(stream)
        stream.append((src, n % RING if slot is None else slot))
        owner_release.append(release)
        return n

    def add_mod(rnd):
        return [add(blk(mods[rnd // 3], 0, (rnd % 3) * 2048 + q * N), ("mod_row", rnd + 1)) for q in range(4)]

    T_X = tiles(["dve"] * 8)
    T_V = tiles(["dve"] * 2)
    B_MOD = {0: add_mod(0)}
    T_PW1 = tiles(["act"] * 16)
    B_PW1 = {}

    def add_pw1(b):
        last = T_PW1 + 8 * b + 8
        B_PW1[b] = (add(blk(A["conv_w_pw1"][0], 0, D + b * N), ("tile_done", last - 1)),
                    add(blk(A["conv_w_pw1"][0], 0, b * N), ("tile_done", last)))

    add_pw1(0)
    B_MOD[1] = add_mod(1)
    add_pw1(1)
    for rnd in range(2, 7):
        B_MOD[rnd] = add_mod(rnd)
    T_PW2 = tiles(["act"] * 8)
    B_PW2 = [add(blk(A["conv_w_pw2"][0], 0, b * N), ("tile_done", T_PW2 + 4 * b + 4)) for b in range(2)]
    T_W1, T_W2, B_W1, B_W2 = {}, {}, {}, {}
    for half in range(2):
        T_W1[half] = tiles(["act"] * 16)
        B_W1[half] = [add(blk(A["mlp_w1"][0], 0, half * 2048 + b * N), ("tile_done", T_W1[half] + 4 * b + 4))
                      for b in range(4)]
        B_MOD[7 + half] = add_mod(7 + half)
        T_W2[half] = tiles(["dve"] * 8)
        B_W2[half] = [add(blk(A["mlp_w2"][0], half * 2048 + kq * D, nh * N), ("tile_done", T_W2[half] + 4 * nh + 4))
                      for nh in range(2) for kq in range(2)]
    T_C = tiles(["dve"] * 8)

    B_IN = []
    units = []
    IN_ORDER = [[("q", i) for i in range(4)],
                [("q", 4), ("q", 5), ("k", 0), ("k", 1), ("c", 0), ("c", 1)],
                [("k", i) for i in range(2, 6)] + [("c", i) for i in range(2, 6)],
                [("v", i) for i in range(NT + CT)],
                [("w", i) for i in range(NT + CT)] + [("f", 0), ("f", 1)]]
    in_tiles = []
    for b, order in enumerate(IN_ORDER):
        for kind, i in order:
            t = tiles(["dve" if kind == "f" else "act"])
            in_tiles.append((b, kind, i, t))
            if kind in "qkc":
                units.append((kind, i, t))
        assert (len(stream) - 58) < 5 and len(stream) >= 58
        B_IN.append(add(blk(A["attn_w_in_2"][0], 0, b * N), ("tile_done", t + 1), 4 + b % 2))
    T_F1 = tiles(["dve"] * 4)
    T_F2 = tiles(["dve"] * 2)
    B_CS = add(blk(A["dft_n"], 0, 0), ("tile_done", T_F2 + 2), 5)
    T_WO = tiles(["dve"] * 8)
    B_WO = [add(blk(A["attn_w_out_2"][0], 0, b * N), ("tile_done", T_WO + 4 * b + 4), 4 + b) for b in range(2)]
    FIRST = len(stream)
    assert FIRST % RING == 0
    T_O = {}
    order_o = []
    T_R, T_H = {}, {}

    def add_route(layer):
        logits_t = tiles(["dve"])
        T_H[layer] = tiles(["dve"] * 8)
        turns = tiles(["dve"] * 3)
        T_R[layer] = [logits_t, turns, turns + 1, turns + 2]

    add_route(0)
    for half in range(2):
        for j in range(4 * half, 4 * half + 4):
            T_O[j] = tiles(["act", "dve", "dve"])
    for half in range(2):
        last = T_O[4 * half + 3]
        for pos, part in enumerate((1, 2, 0)):
            order_o.append((part, half))
            add(blk(A["conv_w_in_2"][0], 0, part * D + half * N), ("tile_done", last + pos + 1))
    T_OO = tiles(["dve"] * 8)
    for b in range(2):
        add(blk(A["conv_w_out_2"][0], 0, b * N), ("tile_done", T_OO + 4 * b + 4))
    add_route(1)
    T_OUT = tiles(["dve"] * 8)
    SECOND = len(stream)
    MOE_BLOCKS = 12 * PAIRS
    loads = [0] * RING
    landed_at = []
    prev = [None] * RING
    prev_of = []
    MOE_LOADS = {}
    for n, (src, slot) in enumerate(stream):
        if n == FIRST:
            MOE_LOADS[0] = list(loads)
            loads = [x + MOE_BLOCKS // RING for x in loads]
        loads[slot] += 1
        landed_at.append((slot, 16 * loads[slot]))
        prev_of.append(prev[slot])
        prev[slot] = n
    MOE_LOADS[1] = list(loads)
    count = {"act": 0, "dve": 0}
    tile_free = []
    for e in tile_by:
        count[e] += 1
        tile_free.append((e, count[e]))

    with ExitStack() as ctx:
        def sb(name, shape, dt=F32):
            return ctx.enter_context(nc.sbuf_tensor(name, shape, dt))

        S = {}

        def sem(name):
            S[name] = ctx.enter_context(nc.semaphore(name))
            return S[name]

        psum = ctx.enter_context(nc.psum_tensor("psum", [P, 8, 512], F32))
        STAT, MISC = 6, 7

        ring = sb("ring", [P, RING * BLK])
        xT = sb("xT", [P, DT, N])
        hT = sb("hT", [P, DT, N])
        arena = sb("arena", [P, 12288])
        K = sb("K", [P, KW])
        vecT = sb("vecT", [P, 5 * P])
        cpad = sb("cpad", [P, DT, 32])
        mod_rows = sb("mod_rows", [P, N])
        mod_raw = sb("mod_raw", [P, 2, 16])
        modv = sb("modv", [P, 4, 48])
        gain = sb("gain", [P, 8, DT])
        gain1 = sb("gain1", [P, DT])
        sq = sb("sq", [P, 2, N])
        rms = sb("rms", [P, N])
        rstd = sb("rstd", [P, N])
        tmp = sb("tmp", [P, 2, N])
        eps = sb("eps", [P, 1])
        one = sb("one", [P, 1])
        gqk = sb("gqk", [P, 3])
        lam_in = sb("lam_in", [P, 4, HD])
        lam_pr = sb("lam_pr", [P, HD])
        lam = sb("lam", [P, 6])
        rw = sb("rw", [P, 2, DT, E])
        small = sb("small", [P, 32])
        logits = sb("logits", [P, NT, E])
        aff = sb("aff", [P, NT, E])
        pos = sb("pos", [P, NT, E])
        top8 = sb("top8", [E, 8])

        def const(name):
            at, w = KCOL[name]
            return K[:, at:at + w]

        ident, cos, sin = const("ident"), const("cos"), const("sin")

        def slot_ap(slot):
            return ring[:, slot * BLK:(slot + 1) * BLK].rearrange("p (k n) -> p k n", k=DT)

        def carve(base, at, *shape):
            n = int(np.prod(shape))
            v = base[:, at:at + n]
            if len(shape) == 2:
                v = v.rearrange("p (a b) -> p a b", a=shape[0])
            if len(shape) == 3:
                v = v.rearrange("p (a b c) -> p a b c", a=shape[0], b=shape[1])
            return v

        vec_rows = carve(arena, DT * SEGS * SEGP, 5, P)
        x_tok = hT[:, :, :].rearrange("p a b -> p (a b)").rearrange("p (t d) -> p t d", t=NT)
        upad = carve(arena, 0, DT, SEGS, SEGP)
        cv = carve(arena, DT * SEGS * SEGP, DT, N)
        glu_a = carve(arena, 10112, 2, N)
        glu_s = carve(arena, 11136, 2, N)
        hid = carve(arena, 0, 16, N)
        ctx_tok = carve(arena, 8192, CT, D)
        xcT = carve(arena, 10240, DT, NC)
        qT = carve(ring, 0, HEADS, N)
        kT = carve(ring, HEADS * N, HEADS, NK)
        vtok = carve(ring, 2 * BLK, NT + CT, QKW)
        fT = carve(ring, 2 * BLK + 4608, 2, N)
        hcT = carve(ring, 2 * BLK + 5632, DT, NC)
        qs = carve(arena, 0, 4, N)
        t_cos = carve(arena, 2048, 2, N)
        t_sin = carve(arena, 3072, 2, N)
        dft1 = carve(arena, 4096, NT, 512)
        prob = carve(arena, 0, 4, NK)
        attn = carve(arena, 3072, 2, NK)
        aT = carve(arena, 4608, HEADS, N)
        o_sb = carve(arena, 7680, N)
        cg = carve(arena, 0, 2, N)
        zpad = carve(arena, 1024, N + 2)
        zc = carve(arena, 1540, N)
        mixed = carve(arena, 2052, DT, N)
        h_tok = carve(arena, 0, NT, D)
        xsT = carve(arena, 4096, DT, P)
        sel = carve(arena, 5120, NT, 2, CAP)
        gsel = carve(arena, 5632, NT, 2, CAP)
        gselT = carve(arena, 6144, N)
        sil = carve(arena, 6656, 2, N)
        act_e = carve(arena, 7680, 2, N)
        aeT = carve(arena, 8704, DT, P)
        y_sb = carve(arena, 9728, D)
        lgT, affT, left = (carve(arena, 10752 + N * m, N)[0:E, :] for m in range(3))
        out_tok = carve(arena, 0, NT, D)

        landed = [sem(f"landed{i}") for i in range(RING)]
        for name in (
            "vec_in", "x_in", "ctx_in", "const_in", "small_in", "stored",
            "tile_done", "act_free", "dve_free", "act_link", "dve_link", "pool_link", "pads_zero",
            "c_silu", "mod_row", "mod_row_sb", "mod_turned", "mod_raw_ready", "mod_ready",
            "sq_ready", "sq_used", "rms_ready", "scaled", "h_ready",
            "u_ready", "conv_done", "mean_done", "mean_sb", "centered",
            "x_pw2", "x_moe", "gains", "hid_ready", "lam_sum", "lam_exp", "qk_in",
            "qk_stat", "qk_rms", "qk_normed", "qk_rot", "qk_done", 
            "scores", "neg_max", "probs", "attn_ready", "attn_turned", "aT_sb", "pv_done", "o_in", "o_stat", "o_rms",
            "o_ready", "cg_ready",
            "soft_exp", "aff_ready", "pos_ready", "acc_zero",
            "sel_ready", "gsel_ready", "gathered", "xs_act", "xs_dve", "gselT_done", "gselT_sb",
            "gate_done", "up_done", "down_done", "sil_ready", "a_ready", "aT_done", "aT_act", "aT_dve",
            "y_act", "y_dve", "scattered", "acc_added",
        ):
            sem(name)
        FREE = {"act": S["act_free"], "dve": S["dve_free"]}

        def emptied(t0):
            return lambda j: (FREE[tile_free[t0 + j][0]], tile_free[t0 + j][1])

        def arrived(eng, n):
            slot, value = landed_at[n]
            eng.wait_ge(landed[slot], value)
            return slot_ap(stream[n][1])

        NORM1, LN, NORM2, FINAL, CTXN, MIX0, FFN0, MIX1, FFN1 = range(9)
        BIASED = {NORM1: 0, LN: 1, NORM2: 2, CTXN: 3, MIX0: 4, FFN0: 5, MIX1: 6, FFN1: 7}

        block = ctx.enter_context(nc.Block())

        @block.sync
        def _(sp):
            def load(n):
                src, slot = stream[n]
                if prev_of[n] is not None:
                    name, value = owner_release[prev_of[n]]
                    sp.wait_ge(S[name], value)
                sp.dma_start(slot_ap(slot), src).then_inc(landed[slot], 16)

            def load_experts(layer):
                for s in range(RING):
                    own = [n for n in range(FIRST if layer == 0 else SECOND) if stream[n][1] == s][-1]
                    name, value = owner_release[own]
                    sp.wait_ge(S[name], value)
                if layer == 0:
                    sp.wait_ge(S["pv_done"], HEADS)
                s0 = 0 if layer == 0 else SECOND % RING
                gate, up, down = (A[f"moe_w_{x}_2"][layer].rearrange("e (k p) n -> e p k n", p=P)
                                  for x in ("gate", "up", "down"))
                with sp.Fori(0, PAIRS) as i:
                    n = i + PAIRS * layer
                    plan = [(gate, 0, "up_done", 2 * n + 1), (gate, 1, "down_done", 2 * n),
                            (up, 0, "down_done", 2 * n + 1), (up, 1, "gate_done", 2 * n + 1),
                            (down, 0, "gate_done", 2 * n + 2), (down, 1, "up_done", 2 * n + 2)]
                    for m, (w, half, name, value) in enumerate(plan):
                        sp.wait_ge(S[name], value)
                        for e in range(2):
                            slot = (s0 + 2 * m + e) % RING
                            src = w[bass.ds(2 * i + e, 1), :, :, half * N:(half + 1) * N]
                            sp.dma_start(slot_ap(slot), src.rearrange("e p k n -> p (e k) n"))\
                                .then_inc(landed[slot], 16)

            for n in range(FIRST):
                load(n)
            load_experts(0)
            for n in range(FIRST, SECOND):
                if prev_of[n] is not None and n < FIRST + RING:
                    sp.wait_ge(S["down_done"], 2 * PAIRS + 1)
                    src, slot = stream[n]
                    sp.dma_start(slot_ap(slot), src).then_inc(landed[slot], 16)
                else:
                    load(n)
            load_experts(1)
            for t in range(NT):
                sp.wait_ge(*emptied(T_OUT)(2 * t + 1))
                sp.dma_start(out[0, t * P:(t + 1) * P, :], out_tok[:, t, :]).then_inc(S["stored"], 16)
            sp.wait_ge(S["stored"], 16 * NT)

        @block.gpsimd
        def _(pool):
            link_n = [0]

            def link(ins):
                link_n[0] += 1
                ins.then_inc(S["pool_link"], 1)
                pool.wait_ge(S["pool_link"], link_n[0])

            pool.memset(cpad[:, :, :], 0.0).then_inc(S["pads_zero"], 1)
            pool.memset(eps[:, :], EPS).then_inc(S["pads_zero"], 1)
            pool.memset(one[:, :], 1.0).then_inc(S["pads_zero"], 1)
            pool.memset(upad[:, :, :, 0:PAD], 0.0).then_inc(S["pads_zero"], 1)
            pool.memset(upad[:, :, :, PAD + SEG:SEGP], 0.0).then_inc(S["pads_zero"], 1)

            def mod_bias(rnd):
                a, r = divmod(rnd, 3)
                pool.wait_ge(S["mod_raw_ready"], rnd + 1)
                bias = vecT[:, COL[f"b_mod{a}"] + 16 * r:COL[f"b_mod{a}"] + 16 * r + 16]
                slots = [[0], [1, 2], [3]][a]
                for m, v in enumerate(slots):
                    ins = pool.tensor_tensor(modv[:, v, 16 * r:16 * r + 16], mod_raw[:, m, :], bias, ALU.add)
                    if v == slots[-1]:
                        ins.then_inc(S["mod_ready"], 1)
                    else:
                        link(ins)
                pool.wait_ge(S["mod_ready"], rnd + 1)

            made = []

            def make_gain(n, v, part, g):
                if made:
                    pool.wait_ge(S["gains"], made[-1])
                link(pool.tensor_scalar(gain1[:, :], modv[:, v, part:part + 8], 1.0, None, ALU.add))
                made.append(len(made) + 1)
                pool.tensor_tensor(gain[:, n, :], gain1[:, :], vecT[:, COL[g[0]] + g[1]:COL[g[0]] + g[1] + 8],
                                   ALU.mult).then_inc(S["gains"], 1)

            def glu(j):
                pool.wait_ge(*emptied(T_PW1 + 2 * j)(1))
                if j == 0:
                    pool.wait_ge(S["pads_zero"], 5)
                pool.tensor_tensor(upad[:, j, :, PAD:PAD + SEG],
                                   glu_a[:, j % 2, :].rearrange("p (s w) -> p s w", s=SEGS),
                                   glu_s[:, j % 2, :].rearrange("p (s w) -> p s w", s=SEGS),
                                   ALU.mult).then_inc(S["u_ready"], 1)

            mod_bias(0)
            make_gain(0, 0, 8, ("norm1_g", 0))
            for j in range(4):
                glu(j)
            glu(4)
            mod_bias(1)
            for j in range(5, 8):
                glu(j)
            mod_bias(2)
            made.append(len(made) + 1)
            pool.tensor_tensor(gain[:, 7, :], modv[:, 0, 16:24], vecT[:, COL["b_pw2"]:COL["b_pw2"] + 8], ALU.mult)\
                .then_inc(S["gains"], 1)
            make_gain(1, 0, 32, ("norm2_g", 0))
            for rnd in range(3, 9):
                mod_bias(rnd)
                if rnd == 5:
                    make_gain(2, 1, 8, ("mix_g", 0))
                    make_gain(3, 2, 8, ("mix_g", 0))
                    make_gain(4, 1, 32, ("ffn_g", 0))
            make_gain(5, 3, 8, ("mix_g", 8))
            make_gain(6, 3, 32, ("ffn_g", 8))
            for layer in range(2):
                pool.wait_ge(*emptied(T_H[layer])(7))
                pool.memset(hT[:, :, :], 0.0).then_inc(S["acc_zero"], 1)

        @block.scalar
        def _(act):
            S_ = S
            g0 = [("c", 0), ("c_2", 8), ("norm2_g", 32), ("norm1_g", 24), ("conv_b_pw1", 48), ("conv_b_dw", 64),
                  ("conv_ln_g", 72), ("conv_ln_b", 80), ("conv_b_pw2", 88)]
            n_vec = 0

            def rows(dst, src):
                nonlocal n_vec
                act.dma_start(dst, src).then_inc(S_["vec_in"], 16)
                n_vec += 1

            act.dma_start(x_tok[:, :, :], A["x"][0].rearrange("(t p) d -> p t d", p=P)).then_inc(S_["x_in"], 16)
            act.dma_start(K[:, :], A["const_k"]).then_inc(S_["const_in"], 16)
            for name, at in g0:
                w = A[name].shape[1] // P
                rows(vec_rows[at:at + w, 0, :], A[name][0].rearrange("(r p) -> r p", p=P))
            for name, at in (("c_ctx_2", 16), ("final_g", 40)):
                rows(vec_rows[at:at + 8, 0, :], A[name].rearrange("(r p) -> r p", p=P))
            for name, at in (("norm_mix_2", 96), ("norm_ffn_2", 112)):
                rows(vec_rows[at:at + 16, 0, :], A[name].rearrange("l (r p) -> (l r) p", p=P))
            rows(vec_rows[0:48, 1, :], A["b_mod"][0].rearrange("(r p) -> r p", p=P))
            rows(vec_rows[48:96, 1, :], A["ada_b_2"][0].rearrange("(r p) -> r p", p=P))
            rows(vec_rows[96:120, 1, :], A["conv_w_2"][0].rearrange("k (r p) -> (k r) p", p=P))
            for m, name in enumerate(("attn_q_norm_2", "attn_k_norm_2")):
                for half in range(2):
                    rows(vec_rows[120 + m:121 + m, 1, half * HD:(half + 1) * HD], A[name])
            rows(vec_rows[122:123, 1, :], A["attn_subln_2"])
            rows(vec_rows[0:48, 2, :], A["ada_b_2"][1].rearrange("(r p) -> r p", p=P))
            taps = A["conv_w_dw"][0].rearrange("k (r p) -> (k r) p", p=P)
            rows(vec_rows[48:128, 2, :], taps[0:80])
            rows(vec_rows[0:128, 3, :], taps[80:208])
            rows(vec_rows[0:40, 4, :], taps[208:248])
            assert n_vec == N_VEC
            for m, name in enumerate(("lam_q1_2", "lam_k1_2", "lam_q2_2", "lam_k2_2")):
                act.dma_start(lam_in[:, m, :], A[name][0].partition_broadcast(P)).then_inc(S_["small_in"], 16)
            for layer in range(2):
                act.dma_start(rw[:, layer, :, :], A["router_w_2"][layer].rearrange("(k p) e -> p k e", p=P))\
                    .then_inc(S_["small_in"], 16)

            link_n = [0]

            def link(ins):
                link_n[0] += 1
                ins.then_inc(S["act_link"], 1)
                act.wait_ge(S["act_link"], link_n[0])

            def squares(n, src, ready, width=N):
                for j in range(DT):
                    g = DT * n + j
                    act.wait_ge(*ready(j))
                    if g >= 2:
                        act.wait_ge(S["sq_used"], g - 1)
                    act.activation(sq[:, g % 2, 0:width], src[:, j, :], ACT.Square).then_inc(S["sq_ready"], 1)

            def root(n, width=N):
                act.wait_ge(S["sq_used"], DT * n + DT)
                if n:
                    act.wait_ge(S["scaled"], DT * n)
                act.activation(rms[:, 0:width], psum[:, STAT, 0:width], ACT.Sqrt, bias=eps[:, 0:1])\
                    .then_inc(S["rms_ready"], 1)

            def shift(n, dst, bias, func=ACT.Identity):
                for j in range(DT):
                    act.wait_ge(S["scaled"], DT * n + j + 1)
                    act.activation(dst[:, j, :], dst[:, j, :], func, bias=bias[:, j:j + 1]).then_inc(S["h_ready"], 1)

            def mod_row(rnd):
                act.wait_ge(S["mod_row"], rnd + 1)
                act.activation(mod_rows[:, :], psum[:, MISC, :], ACT.Copy).then_inc(S["mod_row_sb"], 1)

            def mod_turned(rnd):
                act.wait_ge(S["mod_turned"], rnd + 1)
                if rnd:
                    act.wait_ge(S["mod_ready"], rnd)
                picks = [[0], [1, 2], [1]][rnd // 3]
                view = psum[:, MISC, :].rearrange("p (j q c) -> p q j c", j=4, q=4)
                for m, c in enumerate(picks):
                    act.activation(mod_raw[:, m, :].rearrange("p (q j) -> p q j", q=4), view[:, :, :, c], ACT.Copy)\
                        .then_inc(S["mod_raw_ready" if m == len(picks) - 1 else "act_link"], 1)
                    if m < len(picks) - 1:
                        link_n[0] += 1
                        act.wait_ge(S["act_link"], link_n[0])

            act.sem_inc(S["y_act"], 1)
            act.wait_ge(FREE["dve"], T_V + 2)
            act.wait_ge(S["pads_zero"], 5)
            act.activation(cpad[:, :, 0:3], vecT[:, 0:24].rearrange("p (i k) -> p k i", i=3), ACT.Silu)\
                .then_inc(S["c_silu"], 1)
            squares(NORM1, xT, emptied(T_X))
            root(NORM1)
            mod_row(0)
            mod_turned(0)
            act.wait_ge(S["mod_ready"], 1)
            shift(NORM1, hT, modv[:, 0, 0:8])

            def pw1(j):
                for m, dst in enumerate((glu_s, glu_a)):
                    t = T_PW1 + 2 * j + m
                    act.wait_ge(S["tile_done"], t + 1)
                    if j >= 2:
                        act.wait_ge(S["u_ready"], j - 1)
                    col = COL["b_pw1"] + (8 if m == 0 else 0) + j
                    act.activation(dst[:, j % 2, :], psum[:, t % 6, :], ACT.Sigmoid if m == 0 else ACT.Identity,
                                   bias=vecT[:, col:col + 1]).then_inc(FREE["act"], 1)

            for j in range(4):
                pw1(j)
            mod_row(1)
            pw1(4)
            mod_turned(1)
            for j in range(5, 8):
                pw1(j)
            for rnd in range(2, 7):
                mod_row(rnd)
                mod_turned(rnd)
            act.wait_ge(S["mean_done"], 1)
            act.activation(tmp[:, 0, :], psum[:, STAT, :], ACT.Copy).then_inc(S["mean_sb"], 1)
            squares(LN, cv, lambda j: (S["centered"], j + 1))
            root(LN)
            shift(LN, hT, vecT[:, COL["ln_b"]:COL["ln_b"] + 8], ACT.Silu)
            act.wait_ge(S["gains"], 2)
            for j in range(DT):
                t = T_PW2 + j
                act.wait_ge(S["tile_done"], t + 1)
                if j >= 2:
                    act.wait_ge(S["x_pw2"], j - 1)
                act.activation(tmp[:, j % 2, :], psum[:, t % 6, :], ACT.Identity, bias=gain[:, 7, j:j + 1],
                               scale=modv[:, 0, 16 + j:17 + j]).then_inc(FREE["act"], 1)
            squares(NORM2, xT, lambda j: (S["x_pw2"], j + 1))
            root(NORM2)
            shift(NORM2, hT, modv[:, 0, 24:32])
            act.dma_start(ctx_tok[:, :, :], A["ctx_2"][0].rearrange("(t p) d -> p t d", p=P))\
                .then_inc(S["ctx_in"], 16)
            for half in range(2):
                for m in range(16):
                    t = T_W1[half] + m
                    act.wait_ge(S["tile_done"], t + 1)
                    act.activation(hid[:, m, :], psum[:, t % 6, :], ACT.Relu).then_inc(FREE["act"], 1)
                mod_row(7 + half)
                mod_turned(7 + half)
            squares(FINAL, xT, emptied(T_W2[1]))
            root(FINAL)
            squares(CTXN, xcT, emptied(T_C), NC)
            root(CTXN, NC)
            shift(CTXN, hcT, modv[:, 2, 0:8])
            squares(MIX0, xT, lambda j: (S["scaled"], DT * FINAL + j + 1))
            root(MIX0)
            shift(MIX0, hT, modv[:, 1, 0:8])

            act.wait_ge(S["lam_sum"], 2)
            act.activation(lam[:, 2:4], lam[:, 0:2], ACT.Exp).then_inc(S["lam_exp"], 1)

            def unit_in(u):
                kind, i, t = units[u]
                w = NC if kind == "c" else N
                act.wait_ge(S["tile_done"], t + 1)
                if u >= 4:
                    act.wait_ge(S["qk_done"], u - 3)
                if u >= 2:
                    act.wait_ge(S["qk_stat"], u - 1)
                act.activation(qs[:, u % 4, 0:w], psum[:, t % 6, 0:w], ACT.Copy).then_inc(S["qk_in"], 1)
                act.activation(sq[:, u % 2, 0:w], psum[:, t % 6, 0:w], ACT.Square).then_inc(FREE["act"], 1)

            def unit_root(u):
                w = NC if units[u][0] == "c" else N
                act.wait_ge(S["qk_stat"], u + 1)
                if u:
                    act.wait_ge(S["qk_normed"], u)
                act.activation(rms[:, 0:w], psum[:, STAT, 0:w], ACT.Sqrt, bias=eps[:, 0:1]).then_inc(S["qk_rms"], 1)

            u = 0
            for b, kind, i, t in in_tiles:
                if kind in "qkc":
                    unit_in(u)
                    if u:
                        unit_root(u - 1)
                    u += 1
                elif kind in "vw":
                    if u == len(units):
                        unit_root(u - 1)
                        u += 1
                    act.wait_ge(S["tile_done"], t + 1)
                    if kind == "v":
                        dst, src = vtok[:, i, 0:N], psum[:, t % 6, :]
                    else:
                        dst, src = vtok[:, i, N:QKW], psum[:, t % 6, 0:QKW - N]
                    act.activation(dst, src, ACT.Copy).then_inc(FREE["act"], 1)

            def turn_in(it):
                act.wait_ge(S["attn_turned"], it + 1)
                m = it % 4
                if m == 0 and it:
                    act.wait_ge(S["pv_done"], it // 4)
                act.activation(aT[:, 0:4, m * P:(m + 1) * P], psum[:, 4, :].rearrange("p (a b) -> p a b", a=4),
                               ACT.Copy).then_inc(S["aT_sb"], 1)
                act.activation(aT[:, 4:6, m * P:(m + 1) * P], psum[:, 5, 0:256].rearrange("p (a b) -> p a b", a=2),
                               ACT.Copy).then_inc(S["aT_sb"], 1)

            def head_out(h):
                act.wait_ge(S["pv_done"], h + 1)
                if h:
                    act.wait_ge(S["o_ready"], h)
                act.activation(o_sb, psum[:, STAT, :], ACT.Copy).then_inc(S["o_in"], 1)
                act.activation(sq[:, 0, :], psum[:, STAT, :], ACT.Square).then_inc(S["o_in"], 1)
                act.wait_ge(S["o_stat"], h + 1)
                act.activation(rms[:, :], psum[:, MISC, :], ACT.Sqrt, bias=eps[:, 0:1]).then_inc(S["o_rms"], 1)

            for it in range(4 * HEADS + 1):
                if it < 4 * HEADS:
                    if it >= 2:
                        act.wait_ge(S["attn_ready"], it - 1)
                    for m in range(2):
                        act.wait_ge(S["neg_max"], it + 1)
                        act.activation(prob[:, 2 * (it % 2) + m, :],
                                       psum[:, 2 * m:2 * m + 2, :].rearrange("p a b -> p (a b)")[:, 0:NK], ACT.Exp,
                                       bias=small[:, 2 + m:3 + m],
                                       accum_out=small[:, 4 + 2 * (it % 2) + m:5 + 2 * (it % 2) + m])\
                            .then_inc(S["probs"], 1)
                if it:
                    turn_in(it - 1)
                    if it % 4 == 0:
                        head_out(it // 4 - 1)

            squares(FFN0, xT, emptied(T_WO))
            root(FFN0)
            shift(FFN0, hT, modv[:, 1, 24:32])

            def softmax(layer):
                act.wait_ge(*emptied(T_R[layer][1])(0))
                act.activation(aff[:, :, :], logits[:, :, :], ACT.Exp).then_inc(S["soft_exp"], 1)

            def experts(layer):
                with act.Fori(0, PAIRS) as i:
                    n = i + PAIRS * layer
                    act.wait_ge(S["gathered"], 2 * n + 1)
                    act.activation(xsT[:, 0:4, :], psum[:, 6, :].rearrange("p (a b) -> p a b", a=4), ACT.Copy)\
                        .then_inc(S["xs_act"], 1)
                    act.wait_ge(S["gate_done"], 2 * n + 1)
                    act.wait_ge(S["a_ready"], 2 * n + 1)
                    act.activation(sil[:, 0, :], psum[:, 0, :], ACT.Silu).then_inc(S["sil_ready"], 1)
                    act.wait_ge(S["gselT_done"], n + 2)
                    act.activation(gselT, psum[:, 6, :], ACT.Copy).then_inc(S["gselT_sb"], 1)
                    act.wait_ge(S["gate_done"], 2 * n + 2)
                    act.activation(sil[:, 1, :], psum[:, 1, :], ACT.Silu).then_inc(S["sil_ready"], 1)
                    act.wait_ge(S["aT_done"], 2 * n + 1)
                    act.activation(aeT[:, 0:4, :], psum[:, 6, :].rearrange("p (a b) -> p a b", a=4), ACT.Copy)\
                        .then_inc(S["aT_act"], 1)
                    act.wait_ge(S["down_done"], 2 * n + 2)
                    act.activation(y_sb[:, 0:N], psum[:, 4, :], ACT.Copy).then_inc(S["y_act"], 1)

            softmax(0)
            experts(0)
            squares(MIX1, xT, lambda j: (S["x_moe"], j + 1))
            root(MIX1)
            act.wait_ge(S["mod_ready"], 9)
            shift(MIX1, hT, modv[:, 3, 0:8])
            for j in range(DT):
                t = T_O[j]
                act.wait_ge(S["tile_done"], t + 1)
                if j >= 2:
                    act.wait_ge(*emptied(T_O[j - 2] + 1)(0))
                act.activation(cg[:, j % 2, :], psum[:, t % 6, :], ACT.Copy).then_inc(FREE["act"], 1)
            squares(FFN1, xT, emptied(T_OO))
            root(FFN1)
            shift(FFN1, hT, modv[:, 3, 24:32])
            softmax(1)
            experts(1)

        @block.tensor
        def _(pe):
            def begin(t):
                if t >= 6:
                    e, v = tile_free[t - 6]
                    pe.wait_ge(FREE[e], v)
                return psum[:, t % 6, :]

            def dense(t, w, col, src, kts, width=N, start=True, stop=True, ready=None):
                bank = psum[:, t % 6, :]
                for k in range(kts):
                    if ready is not None:
                        pe.wait_ge(*(ready(k) if callable(ready) else (S[ready[0]], ready[1] + k + 1)))
                    ins = pe.matmul(bank[:, 0:width], w[:, k, col:col + P], src(k), start=start and k == 0,
                                    stop=stop and k == kts - 1)
                return ins

            def turn_tile(t, parts, ready=None):
                bank = begin(t)
                if ready is not None:
                    pe.wait_ge(*ready)
                for m, (src, p) in enumerate(parts):
                    w = src.shape[-1]
                    ins = pe.transpose(bank[0:w, m * P:m * P + p], src, ident[0:p, 0:p])
                ins.then_inc(S["tile_done"], 1)

            def norm_stat(n, width=N):
                if n:
                    pe.wait_ge(S["rms_ready"], n)
                for j in range(DT):
                    g = DT * n + j
                    pe.wait_ge(S["sq_ready"], g + 1)
                    ins = pe.matmul(psum[:, STAT, 0:width], const("ones_d"), sq[:, g % 2, 0:width], start=j == 0,
                                    stop=j == DT - 1)
                    ins.then_inc(S["sq_used"], 1)

            def mod_gemv(rnd):
                ws = [arrived(pe, n) for n in B_MOD[rnd]]
                if rnd == 0:
                    pe.wait_ge(S["c_silu"], 1)
                else:
                    pe.wait_ge(S["mod_raw_ready"], rnd)
                for k in range(DT):
                    for q in range(4):
                        ins = pe.matmul(psum[32 * q:32 * q + 32, MISC, :], cpad[:, k, :], ws[q][:, k, :],
                                        start=k == 0, stop=k == DT - 1, skip_group_check=True)
                ins.then_inc(S["mod_row"], 1)

            def mod_turn(rnd):
                pe.wait_ge(S["mod_row_sb"], rnd + 1)
                for j in range(4):
                    ins = pe.transpose(psum[:, MISC, j * P:(j + 1) * P], mod_rows[:, j * P:(j + 1) * P], ident)
                ins.then_inc(S["mod_turned"], 1)

            for name in ("up_done", "down_done", "gselT_done"):
                pe.sem_inc(S[name], 1)
            pe.wait_ge(S["const_in"], 16)
            pe.wait_ge(S["x_in"], 16)
            for j in range(DT):
                turn_tile(T_X + j, [(x_tok[:, t, j * P:(j + 1) * P], P) for t in range(NT)])
            pe.wait_ge(S["vec_in"], 16 * N_VEC)
            turn_tile(T_V, [(vec_rows[0:VEC_ROWS[g], g, :], VEC_ROWS[g]) for g in range(4)])
            turn_tile(T_V + 1, [(vec_rows[0:VEC_ROWS[4], 4, :], VEC_ROWS[4])])
            norm_stat(NORM1)
            mod_gemv(0)
            mod_turn(0)

            def pw1(j):
                ws = B_PW1[j // 4]
                for m in range(2):
                    t = T_PW1 + 2 * j + m
                    begin(t)
                    w = arrived(pe, ws[m])
                    dense(t, w, (j % 4) * P, lambda k: hT[:, k, :], DT,
                          ready=("h_ready", 0) if j == 0 and m == 0 else None).then_inc(S["tile_done"], 1)

            for j in range(4):
                pw1(j)
            mod_gemv(1)
            pw1(4)
            mod_turn(1)
            for j in range(5, 8):
                pw1(j)
            for rnd in range(2, 7):
                mod_gemv(rnd)
                mod_turn(rnd)
            pe.wait_ge(S["rms_ready"], 1)
            for j in range(DT):
                pe.wait_ge(S["conv_done"], j + 1)
                ins = pe.matmul(psum[:, STAT, :], const("ones_d"), cv[:, j, :], start=j == 0, stop=j == DT - 1)
            ins.then_inc(S["mean_done"], 1)
            pe.wait_ge(S["mean_sb"], 1)
            norm_stat(LN)
            for j in range(DT):
                t = T_PW2 + j
                begin(t)
                w = arrived(pe, B_PW2[j // 4])
                dense(t, w, (j % 4) * P, lambda k: hT[:, k, :], DT,
                      ready=("h_ready", 8) if j == 0 else None).then_inc(S["tile_done"], 1)
            norm_stat(NORM2)
            for half in range(2):
                for m in range(16):
                    t = T_W1[half] + m
                    begin(t)
                    w = arrived(pe, B_W1[half][m // 4])
                    dense(t, w, (m % 4) * P, lambda k: hT[:, k, :], DT,
                          ready=("h_ready", 16) if (half, m) == (0, 0) else None).then_inc(S["tile_done"], 1)
                mod_gemv(7 + half)
                for nh in range(2):
                    for kq in range(2):
                        w = arrived(pe, B_W2[half][2 * nh + kq])
                        for j in range(4):
                            t = T_W2[half] + 4 * nh + j
                            if kq == 0:
                                begin(t)
                            ins = dense(t, w, j * P, lambda k: hid[:, 8 * kq + k, :], DT, start=kq == 0, stop=kq == 1,
                                        ready=("hid_ready", 16 * half + 8 * kq) if nh == 0 and j == 0 else None)
                            if kq == 1:
                                ins.then_inc(S["tile_done"], 1)
                        if nh == 0 and kq == 0:
                            mod_turn(7 + half)
            pe.wait_ge(S["ctx_in"], 16)
            for j in range(DT):
                turn_tile(T_C + j, [(ctx_tok[:, t, j * P:(j + 1) * P], P) for t in range(CT)])
            norm_stat(FINAL)
            norm_stat(CTXN, NC)
            norm_stat(MIX0)

            def unit_stat(u):
                w = NC if units[u][0] == "c" else N
                pe.wait_ge(FREE["act"], tile_free[units[u][2]][1])
                if u:
                    pe.wait_ge(S["qk_rms"], u)
                else:
                    pe.wait_ge(S["rms_ready"], MIX0 + 1)
                pe.matmul(psum[:, STAT, 0:w], const("ones_h"), sq[:, u % 2, 0:w], start=True, stop=True)\
                    .then_inc(S["qk_stat"], 1)

            rotated = [0]

            def unit_rotate(u):
                if units[u][0] == "c":
                    return
                pe.wait_ge(S["qk_normed"], u + 1)
                if rotated[0]:
                    last = [v for v in range(u) if units[v][0] != "c"][-1]
                    pe.wait_ge(S["qk_done"], last + 1)
                rotated[0] += 1
                pe.matmul(psum[:, MISC, :], const("rope"), qs[:, u % 4, :], start=True, stop=True)\
                    .then_inc(S["qk_rot"], 1)

            u = 0
            first = True
            for b, kind, i, t in in_tiles:
                begin(t)
                w = arrived(pe, B_IN[b])
                if kind in "qkf":
                    col = {"q": i * P, "k": QKW + i * P, "f": 2 * QKW + QKW + i * P}[kind] - b * N
                    ins = dense(t, w, col, lambda k: hT[:, k, :], DT, ready=("h_ready", 32) if first else None)
                    first = False
                elif kind == "c":
                    ins = dense(t, w, QKW + i * P - b * N, lambda k: hcT[:, k, :], DT, width=NC)
                else:
                    width = N if kind == "v" else QKW - N
                    for k in range(DT):
                        src = hT[:, k, i * P:(i + 1) * P] if i < NT else hcT[:, k, (i - NT) * P:(i - NT + 1) * P]
                        ins = pe.matmul(psum[:, t % 6, 0:width], src, w[:, k, 0:width], start=k == 0, stop=k == DT - 1)
                ins.then_inc(S["tile_done"], 1)
                if kind in "qkc":
                    if u >= 1:
                        unit_stat(u - 1)
                    if u >= 2:
                        unit_rotate(u - 2)
                    u += 1
                elif kind == "v" and i < 2:
                    if i == 0:
                        unit_stat(u - 1)
                        unit_rotate(u - 2)
                    else:
                        unit_rotate(u - 1)
            for t in range(NT):
                begin(T_F1 + t)
                pe.wait_ge(*emptied(in_tiles[-1][3])(0))
                for ft in range(2):
                    ins = pe.matmul(psum[:, (T_F1 + t) % 6, 256 * ft:256 * ft + 256], fT[:, ft, t * P:(t + 1) * P],
                                    const("dft_d"), start=ft == 0, stop=ft == 1, skip_group_check=True)
                ins.then_inc(S["tile_done"], 1)
            w = arrived(pe, B_CS)
            for ft in range(2):
                begin(T_F2 + ft)
                pe.wait_ge(*emptied(T_F1)(3))
                for m in range(2 * NT):
                    t, part = m % NT, m // NT
                    ins = pe.matmul(psum[:, (T_F2 + ft) % 6, :], dft1[:, t, 256 * ft + P * part:256 * ft + P * part + P],
                                    w[:, m, :], start=m == 0, stop=m == 2 * NT - 1)
                ins.then_inc(S["tile_done"], 1)

            for e in ("act", "dve"):
                pe.wait_ge(FREE[e], [v for x, v in tile_free[:T_F2 + 2] if x == e][-1])
            pe.wait_ge(S["qk_done"], len(units))

            def scores(it):
                h, m = divmod(it, 4)
                if it:
                    pe.wait_ge(S["probs"], 2 * it)
                for lo, hi, off in ((0, 512, 0), (512, NK, 1)):
                    for c in range(2):
                        ins = pe.matmul(psum[:, 2 * c + off, 0:hi - lo], qT[64 * c:64 * c + 64, h, m * P:(m + 1) * P],
                                        kT[64 * c:64 * c + 64, h, lo:hi], start=True, stop=True)
                ins.then_inc(S["scores"], 1)

            def attn_turn(it):
                pe.wait_ge(S["attn_ready"], it + 1)
                if it:
                    pe.wait_ge(S["aT_sb"], 2 * it)
                for k in range(6):
                    ins = pe.transpose(psum[:, 4 + k // 4, (k % 4) * P:(k % 4 + 1) * P],
                                       attn[:, it % 2, k * P:(k + 1) * P], ident)
                ins.then_inc(S["attn_turned"], 1)

            def values(h):
                pe.wait_ge(S["aT_sb"], 8 * h + 8)
                if h:
                    pe.wait_ge(S["o_in"], 2 * h)
                for k in range(6):
                    ins = pe.matmul(psum[:, STAT, :], vtok[:, k, h * P:(h + 1) * P], aT[:, k, :], start=k == 0,
                                    stop=k == 5)
                ins.then_inc(S["pv_done"], 1)

            def head_stat(h):
                pe.wait_ge(S["o_in"], 2 * h + 2)
                if h:
                    pe.wait_ge(S["o_rms"], h)
                pe.matmul(psum[:, MISC, :], const("ones_v"), sq[:, 0, :], start=True, stop=True)\
                    .then_inc(S["o_stat"], 1)

            scores(0)
            for it in range(4 * HEADS):
                if it + 1 < 4 * HEADS:
                    scores(it + 1)
                attn_turn(it)
                if it % 4 == 3:
                    values(it // 4)
                    head_stat(it // 4)
            for j in range(DT):
                t = T_WO + j
                if j == 0:
                    pe.wait_ge(S["aT_sb"], 8 * HEADS)
                    pe.wait_ge(S["o_rms"], HEADS)
                    pe.wait_ge(S["o_ready"], HEADS)
                else:
                    begin(t)
                w = arrived(pe, B_WO[j // 4])
                dense(t, w, (j % 4) * P, lambda k: hT[:, k, :], DT).then_inc(S["tile_done"], 1)
            norm_stat(FFN0)

            def route(layer):
                n = FFN0 if layer == 0 else FFN1
                t = T_R[layer][0]
                begin(t)
                for k in range(DT):
                    pe.wait_ge(S["h_ready"], 8 * BIASED[n] + k + 1)
                    ins = pe.matmul(psum[0:E, t % 6, :], rw[:, layer, k, :], hT[:, k, :], start=k == 0, stop=k == DT - 1)
                ins.then_inc(S["tile_done"], 1)
                for m in range(8):
                    tt, half = divmod(m, 2)
                    turn_tile(T_H[layer] + m, [(hT[:, 4 * half + j, tt * P:(tt + 1) * P], P) for j in range(4)])
                t = T_R[layer][1] - 1
                pe.wait_ge(FREE["dve"], tile_free[T_R[layer][0]][1])
                begin(t + 1)
                for m in range(NT):
                    ins = pe.transpose(psum[:, (t + 1) % 6, m * E:(m + 1) * E], lgT[:, m * P:(m + 1) * P],
                                       ident[0:E, 0:E])
                ins.then_inc(S["tile_done"], 1)
                pe.wait_ge(S["aff_ready"], layer + 1)
                begin(t + 2)
                for m in range(NT):
                    ins = pe.transpose(psum[0:E, (t + 2) % 6, m * P:(m + 1) * P], aff[:, m, :], ident)
                ins.then_inc(S["tile_done"], 1)
                pe.wait_ge(S["pos_ready"], layer + 1)
                begin(t + 3)
                for m in range(NT):
                    ins = pe.transpose(psum[:, (t + 3) % 6, m * E:(m + 1) * E], left[:, m * P:(m + 1) * P],
                                       ident[0:E, 0:E])
                ins.then_inc(S["tile_done"], 1)

            def experts(layer):
                s0 = 0 if layer == 0 else SECOND % RING
                t = T_R[layer][3]
                for e in ("act", "dve"):
                    pe.wait_ge(FREE[e], [v for x, v in tile_free[:t + 1] if x == e][-1])
                with pe.Fori(0, PAIRS) as i:
                    n = i + PAIRS * layer

                    def pair(m):
                        got = []
                        for e in range(2):
                            slot = (s0 + 2 * m + e) % RING
                            before = MOE_LOADS[layer][slot]
                            pe.wait_ge(landed[slot], 32 * i + 16 * (before + (2 * m + e) // RING + 1))
                            got.append(slot_ap(slot))
                        return got

                    def products(bank, m, src, name):
                        wa, wb = pair(m)
                        for k in range(DT):
                            for e, w in enumerate((wa, wb)):
                                ins = pe.matmul(psum[64 * e:64 * e + 64, bank, :], src[:, k, 64 * e:64 * e + 64],
                                                w[:, k, :], start=k == 0, stop=k == DT - 1, skip_group_check=True)
                        ins.then_inc(S[name], 1)

                    pe.wait_ge(S["sel_ready"], n + 1)
                    pe.wait_ge(S["acc_added"], 8 * n + 1)
                    for fj in range(DT):
                        for tt in range(NT):
                            ins = pe.matmul(psum[:, 6 + fj // 4, (fj % 4) * P:(fj % 4 + 1) * P],
                                            h_tok[:, tt, fj * P:(fj + 1) * P],
                                            sel[:, tt, :, :].rearrange("p a b -> p (a b)"),
                                            start=tt == 0, stop=tt == NT - 1)
                        if fj % 4 == 3:
                            ins.then_inc(S["gathered"], 1)
                    pe.wait_ge(S["xs_act"], n + 1)
                    pe.wait_ge(S["xs_dve"], n + 1)
                    pe.wait_ge(S["a_ready"], 2 * n + 1)
                    products(0, 0, xsT, "gate_done")
                    pe.wait_ge(S["gsel_ready"], n + 1)
                    for tt in range(NT):
                        ins = pe.transpose(psum[:, 6, tt * P:(tt + 1) * P],
                                           gsel[:, tt, :, :].rearrange("p a b -> p (a b)"), ident)
                    ins.then_inc(S["gselT_done"], 1)
                    products(1, 1, xsT, "gate_done")
                    products(2, 2, xsT, "up_done")
                    products(3, 3, xsT, "up_done")
                    pe.wait_ge(S["gselT_sb"], n + 1)
                    for half in range(2):
                        pe.wait_ge(S["a_ready"], 2 * n + 2 + half)
                        for j in range(4):
                            ins = pe.transpose(psum[:, 6 + half, j * P:(j + 1) * P],
                                               act_e[:, half, j * P:(j + 1) * P], ident)
                        ins.then_inc(S["aT_done"], 1)
                    pe.wait_ge(S["aT_act"], n + 1)
                    pe.wait_ge(S["aT_dve"], n + 1)
                    pe.wait_ge(S["y_act"], n + 1)
                    pe.wait_ge(S["y_dve"], n + 1)
                    products(4, 4, aeT, "down_done")
                    products(5, 5, aeT, "down_done")
                    pe.wait_ge(S["y_act"], n + 2)
                    for fj in range(DT):
                        if fj >= 2:
                            pe.wait_ge(S["acc_added"], 8 * n + fj)
                        if fj == 4:
                            pe.wait_ge(S["y_dve"], n + 2)
                        pe.matmul(psum[:, 6 + fj % 2, :], y_sb[:, fj * P:(fj + 1) * P], gselT, start=True, stop=True)\
                            .then_inc(S["scattered"], 1)

            route(0)
            experts(0)
            norm_stat(MIX1)
            oo = FIRST

            def mixed_at(k):
                return emptied(T_O[k] + 2)(0)

            for j in range(DT):
                for m in range(3):
                    t = T_O[j] + m
                    begin(t)
                    w = arrived(pe, oo + 3 * (j // 4) + m)
                    dense(t, w, (j % 4) * P, lambda k: hT[:, k, :], DT,
                          ready=("h_ready", 8 * BIASED[MIX1]) if (j, m) == (0, 0) else None)\
                        .then_inc(S["tile_done"], 1)
            for j in range(DT):
                t = T_OO + j
                begin(t)
                w = arrived(pe, oo + 6 + j // 4)
                dense(t, w, (j % 4) * P, lambda k: mixed[:, k, :], DT,
                      ready=mixed_at if j == 0 else None).then_inc(S["tile_done"], 1)
            norm_stat(FFN1)
            route(1)
            experts(1)
            for m in range(8):
                tt, half = divmod(m, 2)
                turn_tile(T_OUT + m, [(xT[:, 4 * half + j, tt * P:(tt + 1) * P], P) for j in range(4)],
                          ready=(S["x_moe"], 16))

        @block.vector
        def _(dve):
            link_n = [0]

            def link(ins):
                link_n[0] += 1
                ins.then_inc(S["dve_link"], 1)
                dve.wait_ge(S["dve_link"], link_n[0])

            def scale(n, src, dst, gains, width=N):
                if n:
                    dve.wait_ge(S["scaled"], DT * n)
                dve.wait_ge(S["rms_ready"], n + 1)
                link(dve.reciprocal(rstd[:, 0:width], rms[:, 0:width]))
                for j in range(DT):
                    ins = dve.scalar_tensor_tensor(out=dst[:, j, :], in0=src[:, j, :], scalar=gains[:, j:j + 1],
                                                   in1=rstd[:, 0:width], op0=ALU.mult, op1=ALU.mult)
                    ins.then_inc(S["scaled"], 1)

            def vec(name, off=0):
                return vecT[:, COL[name] + off:COL[name] + off + 8]

            def add_to_x(t, g, j):
                dve.wait_ge(S["tile_done"], t + 1)
                dve.scalar_tensor_tensor(out=xT[:, j, :], in0=psum[:, t % 6, :], scalar=g[:, j:j + 1],
                                         in1=xT[:, j, :], op0=ALU.mult, op1=ALU.add).then_inc(FREE["dve"], 1)

            for name in ("a_ready", "y_dve", "acc_added"):
                dve.sem_inc(S[name], 1)
            for j in range(DT):
                dve.wait_ge(S["tile_done"], T_X + j + 1)
                dve.tensor_copy(xT[:, j, :], psum[:, (T_X + j) % 6, :]).then_inc(FREE["dve"], 1)
            dve.wait_ge(S["tile_done"], T_V + 1)
            for g in range(4):
                w = VEC_ROWS[g]
                ins = dve.tensor_copy(vecT[:, g * P:g * P + w], psum[:, T_V % 6, g * P:g * P + w])
                if g < 3:
                    link(ins)
            ins.then_inc(FREE["dve"], 1)
            dve.wait_ge(S["tile_done"], T_V + 2)
            dve.tensor_copy(vecT[:, 4 * P:4 * P + VEC_ROWS[4]], psum[:, (T_V + 1) % 6, 0:VEC_ROWS[4]])\
                .then_inc(FREE["dve"], 1)
            dve.wait_ge(FREE["dve"], T_V + 2)
            dve.tensor_scalar(gqk[:, 0:1], vecT[:, COL["q_g"]:COL["q_g"] + 1], HD ** -0.5, None, ALU.mult)
            dve.tensor_copy(gqk[:, 1:2], vecT[:, COL["k_g"]:COL["k_g"] + 1])
            link(dve.tensor_scalar(gqk[:, 2:3], vecT[:, COL["subln"]:COL["subln"] + 1], 1.0 - LAM_INIT, None, ALU.mult))
            dve.wait_ge(S["small_in"], 16 * 6)
            for m in range(2):
                dve.tensor_tensor_reduce(out=lam_pr[:, :], in0=lam_in[:, 2 * m, :], in1=lam_in[:, 2 * m + 1, :],
                                         scale=1.0, scalar=0.0, op0=ALU.mult, op1=ALU.add,
                                         accum_out=lam[:, m:m + 1]).then_inc(S["lam_sum"], 1)
                dve.wait_ge(S["lam_sum"], m + 1)
            dve.wait_ge(S["gains"], 1)
            scale(NORM1, xT, hT, gain[:, 0, :])

            for j in range(DT):
                dve.wait_ge(S["u_ready"], j + 1)
                acc = cv[:, j, :].rearrange("p (s w) -> p s w", s=SEGS)
                for k in range(TAPS):
                    w = vecT[:, COL["w_dw"] + k * 8 + j:COL["w_dw"] + k * 8 + j + 1]
                    u = upad[:, j, :, k:k + SEG]
                    if k == 0:
                        ins = dve.tensor_scalar(acc, u, w, vecT[:, COL["b_dw"] + j:COL["b_dw"] + j + 1], ALU.mult,
                                                ALU.add)
                    else:
                        ins = dve.scalar_tensor_tensor(out=acc, in0=u, scalar=w, in1=acc, op0=ALU.mult, op1=ALU.add)
                    if k < TAPS - 1:
                        link(ins)
                ins.then_inc(S["conv_done"], 1)
            dve.wait_ge(S["conv_done"], DT)
            dve.wait_ge(S["mean_sb"], 1)
            for j in range(DT):
                dve.tensor_tensor(cv[:, j, :], cv[:, j, :], tmp[:, 0, :], ALU.subtract).then_inc(S["centered"], 1)
            dve.wait_ge(S["centered"], DT)
            scale(LN, cv, hT, vec("ln_g"))
            for j in range(DT):
                dve.wait_ge(FREE["act"], tile_free[T_PW2 + j][1])
                dve.tensor_tensor(xT[:, j, :], xT[:, j, :], tmp[:, j % 2, :], ALU.add).then_inc(S["x_pw2"], 1)
            dve.wait_ge(S["gains"], 3)
            scale(NORM2, xT, hT, gain[:, 1, :])
            for half in range(2):
                for m in range(16):
                    dve.wait_ge(FREE["act"], tile_free[T_W1[half] + m][1])
                    dve.tensor_tensor(hid[:, m, :], hid[:, m, :], hid[:, m, :], ALU.mult).then_inc(S["hid_ready"], 1)
                for j in range(DT):
                    add_to_x(T_W2[half] + j, modv[:, 0, 40:48], j)
            for j in range(DT):
                t = T_C + j
                dve.wait_ge(S["tile_done"], t + 1)
                dve.tensor_copy(xcT[:, j, :], psum[:, t % 6, 0:NC]).then_inc(FREE["dve"], 1)
            scale(FINAL, xT, xT, vec("final_g"))
            dve.wait_ge(FREE["dve"], tile_free[T_C + 7][1])
            dve.wait_ge(S["gains"], 8)
            scale(CTXN, xcT, hcT, gain[:, 3, :], NC)
            scale(MIX0, xT, hT, gain[:, 2, :])

            dve.wait_ge(S["lam_exp"], 1)
            link(dve.tensor_tensor(lam[:, 4:5], lam[:, 3:4], lam[:, 2:3], ALU.subtract))
            link(dve.tensor_scalar(lam[:, 5:6], lam[:, 4:5], -LAM_INIT, None, ALU.add))

            def unit_norm(u):
                kind, i, t = units[u]
                w = NC if kind == "c" else N
                dve.wait_ge(S["qk_rms"], u + 1)
                link(dve.reciprocal(rstd[:, 0:w], rms[:, 0:w]))
                g = gqk[:, 0:1] if kind == "q" else gqk[:, 1:2]
                dst = kT[:, i, N:NK] if kind == "c" else qs[:, u % 4, :]
                dve.scalar_tensor_tensor(out=dst, in0=qs[:, u % 4, 0:w], scalar=g, in1=rstd[:, 0:w], op0=ALU.mult,
                                         op1=ALU.mult).then_inc(S["qk_normed"], 1)
                dve.wait_ge(S["qk_normed"], u + 1)

            rot = [0]

            def unit_done(u):
                kind, i, t = units[u]
                if kind == "c":
                    dve.nop().then_inc(S["qk_done"], 1)
                    return
                dst = qT[:, i, :] if kind == "q" else kT[:, i, 0:N]
                b = rot[0] % 2
                rot[0] += 1
                dve.tensor_tensor(t_cos[:, b, :], qs[:, u % 4, :], cos, ALU.mult)
                dve.wait_ge(S["qk_rot"], rot[0])
                link(dve.tensor_tensor(t_sin[:, b, :], psum[:, MISC, :], sin, ALU.mult))
                dve.tensor_tensor(dst, t_cos[:, b, :], t_sin[:, b, :], ALU.add).then_inc(S["qk_done"], 1)
                dve.wait_ge(S["qk_done"], u + 1)

            for u in range(len(units) + 1):
                if u < len(units):
                    unit_norm(u)
                if u >= 1:
                    unit_done(u - 1)
            for b, kind, i, t in in_tiles:
                if kind == "f":
                    dve.wait_ge(S["tile_done"], t + 1)
                    dve.tensor_copy(fT[:, i, :], psum[:, t % 6, :]).then_inc(FREE["dve"], 1)
            for t in range(NT):
                dve.wait_ge(S["tile_done"], T_F1 + t + 1)
                dve.tensor_copy(dft1[:, t, :], psum[:, (T_F1 + t) % 6, :]).then_inc(FREE["dve"], 1)
            for ft in range(2):
                dve.wait_ge(S["tile_done"], T_F2 + ft + 1)
                dve.tensor_copy(hT[:, HEADS + ft, :], psum[:, (T_F2 + ft) % 6, :]).then_inc(FREE["dve"], 1)

            def softmax_max(it):
                dve.wait_ge(S["scores"], it + 1)
                link(dve.tensor_reduce(small[:, 0:2],
                                       psum[:, 0:4, :].rearrange("p (c a) b -> p c (a b)", c=2)[:, :, 0:NK],
                                       AX.X, ALU.max))
                if it:
                    dve.wait_ge(S["probs"], 2 * it)
                dve.tensor_scalar(small[:, 2:4], small[:, 0:2], -1.0, None, ALU.mult).then_inc(S["neg_max"], 1)

            def combine(it):
                b = it % 2
                dve.wait_ge(S["probs"], 2 * it + 2)
                link(dve.reciprocal(small[:, 8 + 4 * b:10 + 4 * b], small[:, 4 + 2 * b:6 + 2 * b]))
                link(dve.tensor_scalar(small[:, 10 + 4 * b:11 + 4 * b], small[:, 9 + 4 * b:10 + 4 * b], lam[:, 5:6],
                                       None, ALU.mult))
                link(dve.tensor_scalar(prob[:, 2 * b + 1, :], prob[:, 2 * b + 1, :], small[:, 10 + 4 * b:11 + 4 * b],
                                       None, ALU.mult))
                if it >= 2:
                    dve.wait_ge(S["attn_turned"], it - 1)
                dve.scalar_tensor_tensor(out=attn[:, b, :], in0=prob[:, 2 * b, :], scalar=small[:, 8 + 4 * b:9 + 4 * b],
                                         in1=prob[:, 2 * b + 1, :], op0=ALU.mult, op1=ALU.add)\
                    .then_inc(S["attn_ready"], 1)

            def head_norm(h):
                dve.wait_ge(S["o_rms"], h + 1)
                link(dve.reciprocal(rstd[:, :], rms[:, :]))
                dve.scalar_tensor_tensor(out=hT[:, h, :], in0=o_sb, scalar=gqk[:, 2:3], in1=rstd[:, :], op0=ALU.mult,
                                         op1=ALU.mult).then_inc(S["o_ready"], 1)
                dve.wait_ge(S["o_ready"], h + 1)

            softmax_max(0)
            for it in range(4 * HEADS):
                combine(it)
                if it + 1 < 4 * HEADS:
                    softmax_max(it + 1)
                if it % 4 == 3:
                    head_norm(it // 4)
            for j in range(DT):
                add_to_x(T_WO + j, modv[:, 1, 16:24], j)
            scale(FFN0, xT, hT, gain[:, 4, :])

            def route_all(layer):
                t = T_R[layer][1] - 1
                lt = logits[:, :, :]

                def wide(ap):
                    return ap.unsqueeze(2).to_broadcast([P, NT, E])

                t0 = T_R[layer][0]
                dve.wait_ge(S["tile_done"], t0 + 1)
                dve.tensor_copy(lgT[:, :], psum[0:E, t0 % 6, :]).then_inc(FREE["dve"], 1)
                for m in range(8):
                    tt, half = divmod(m, 2)
                    dve.wait_ge(S["tile_done"], T_H[layer] + m + 1)
                    dve.tensor_copy(h_tok[:, tt, half * N:(half + 1) * N], psum[:, (T_H[layer] + m) % 6, :])\
                        .then_inc(FREE["dve"], 1)
                dve.wait_ge(S["tile_done"], t + 2)
                ps = psum[:, (t + 1) % 6, 0:NT * E].rearrange("p (a b) -> p a b", a=NT)
                link(dve.tensor_reduce(small[:, 16:20], ps, AX.X, ALU.max))
                dve.tensor_tensor(lt, ps, wide(small[:, 16:20]), ALU.subtract).then_inc(FREE["dve"], 1)
                dve.wait_ge(S["soft_exp"], layer + 1)
                link(dve.tensor_reduce(small[:, 20:24], aff[:, :, :], AX.X, ALU.add))
                link(dve.reciprocal(small[:, 24:28], small[:, 20:24]))
                dve.tensor_tensor(aff[:, :, :], aff[:, :, :], wide(small[:, 24:28]), ALU.mult)\
                    .then_inc(S["aff_ready"], 1)
                dve.wait_ge(S["tile_done"], t + 3)
                dve.tensor_copy(left[:, :], psum[0:E, (t + 2) % 6, :]).then_inc(FREE["dve"], 1)
                dve.wait_ge(FREE["dve"], tile_free[t + 2][1])
                for r in range(CAP // 8):
                    link(dve.max(top8[:, :], left[:, :]))
                    link(dve.match_replace(left[:, :], top8[:, :], left[:, :], -1.0))
                link(dve.tensor_scalar(affT[:, :], left[:, :], 0.0, None, ALU.is_lt))
                link(dve.tensor_tensor_scan(lgT[:, :], one[0:E, :].to_broadcast([E, N]), affT[:, :], 0.0, ALU.mult,
                                            ALU.add))
                dve.tensor_tensor(left[:, :], lgT[:, :], affT[:, :], ALU.mult).then_inc(S["pos_ready"], 1)
                dve.wait_ge(S["tile_done"], t + 4)
                dve.tensor_copy(pos[:, :, :], psum[:, (t + 3) % 6, 0:NT * E].rearrange("p (a b) -> p a b", a=NT))\
                    .then_inc(FREE["dve"], 1)
                dve.wait_ge(FREE["dve"], tile_free[t + 3][1])
                dve.wait_ge(S["acc_zero"], layer + 1)

            def experts(layer):
                iota = const("iota").unsqueeze(1).unsqueeze(1).to_broadcast([P, NT, 2, CAP])

                def each(src, i):
                    return src[:, :, bass.ds(2 * i, 2)].unsqueeze(3).to_broadcast([P, NT, 2, CAP])

                with dve.Fori(0, PAIRS) as i:
                    n = i + PAIRS * layer
                    dve.wait_ge(S["gselT_done"], n + 1)
                    dve.tensor_tensor(sel, iota, each(pos, i), ALU.is_equal).then_inc(S["sel_ready"], 1)
                    dve.wait_ge(S["sel_ready"], n + 1)
                    dve.tensor_tensor(gsel, sel, each(aff, i), ALU.mult).then_inc(S["gsel_ready"], 1)
                    dve.wait_ge(S["gathered"], 2 * n + 2)
                    dve.tensor_copy(xsT[:, 4:8, :], psum[:, 7, :].rearrange("p (a b) -> p a b", a=4))\
                        .then_inc(S["xs_dve"], 1)
                    for half in range(2):
                        dve.wait_ge(S["up_done"], 2 * n + 2 + half)
                        dve.wait_ge(S["sil_ready"], 2 * n + 1 + half)
                        dve.tensor_tensor(act_e[:, half, :], psum[:, 2 + half, :], sil[:, half, :], ALU.mult)\
                            .then_inc(S["a_ready"], 1)
                    dve.wait_ge(S["aT_done"], 2 * n + 2)
                    dve.tensor_copy(aeT[:, 4:8, :], psum[:, 7, :].rearrange("p (a b) -> p a b", a=4))\
                        .then_inc(S["aT_dve"], 1)
                    dve.wait_ge(S["down_done"], 2 * n + 3)
                    dve.tensor_copy(y_sb[:, N:D], psum[:, 5, :]).then_inc(S["y_dve"], 1)
                    for fj in range(DT):
                        dve.wait_ge(S["scattered"], 8 * n + fj + 1)
                        dve.tensor_tensor(hT[:, fj, :], hT[:, fj, :], psum[:, 6 + fj % 2, :], ALU.add)\
                            .then_inc(S["acc_added"], 1)
                v = 1 if layer == 0 else 3
                dve.wait_ge(S["acc_added"], 8 * PAIRS * (layer + 1) + 1)
                for j in range(DT):
                    dve.scalar_tensor_tensor(out=xT[:, j, :], in0=hT[:, j, :], scalar=modv[:, v, 40 + j:41 + j],
                                             in1=xT[:, j, :], op0=ALU.mult, op1=ALU.add).then_inc(S["x_moe"], 1)
                dve.wait_ge(S["x_moe"], 8 * layer + 8)

            route_all(0)
            experts(0)
            scale(MIX1, xT, hT, gain[:, 5, :])
            dve.memset(zpad[:, 0:1], 0.0)
            link(dve.memset(zpad[:, N + 1:N + 2], 0.0))
            for j in range(DT):
                t = T_O[j]
                dve.wait_ge(S["tile_done"], t + 2)
                dve.wait_ge(FREE["act"], tile_free[t][1])
                dve.tensor_tensor(zpad[:, 1:N + 1], psum[:, (t + 1) % 6, :], cg[:, j % 2, :], ALU.mult)\
                    .then_inc(FREE["dve"], 1)
                dve.wait_ge(FREE["dve"], tile_free[t + 1][1])
                for k in range(3):
                    w = vecT[:, COL["w_conv3"] + 8 * k + j:COL["w_conv3"] + 8 * k + j + 1]
                    if k == 0:
                        link(dve.tensor_scalar(zc, zpad[:, 0:N], w, None, ALU.mult))
                    else:
                        link(dve.scalar_tensor_tensor(out=zc, in0=zpad[:, k:k + N], scalar=w, in1=zc, op0=ALU.mult,
                                                      op1=ALU.add))
                dve.wait_ge(S["tile_done"], t + 3)
                dve.tensor_tensor(mixed[:, j, :], psum[:, (t + 2) % 6, :], zc, ALU.mult).then_inc(FREE["dve"], 1)
            for j in range(DT):
                add_to_x(T_OO + j, modv[:, 3, 16:24], j)
            scale(FFN1, xT, hT, gain[:, 6, :])
            route_all(1)
            experts(1)
            for m in range(8):
                tt, half = divmod(m, 2)
                t = T_OUT + m
                dve.wait_ge(S["tile_done"], t + 1)
                dve.tensor_copy(out_tok[:, tt, half * N:(half + 1) * N], psum[:, t % 6, :]).then_inc(FREE["dve"], 1)


_INS = ["x", "c", "w_mod", "b_mod", "norm1_g", "norm2_g", "final_g", "conv_w_pw1", "conv_b_pw1", "conv_w_dw",
        "conv_b_dw", "conv_ln_g", "conv_ln_b", "conv_w_pw2", "conv_b_pw2", "mlp_w1", "mlp_w2", "c_2", "ctx_2",
        "c_ctx_2", "ada_w_2", "ada_b_2", "norm_mix_2", "norm_ffn_2", "attn_w_in_2", "attn_q_norm_2",
        "attn_k_norm_2", "lam_q1_2", "lam_k1_2", "lam_q2_2", "lam_k2_2", "attn_subln_2", "attn_w_out_2",
        "conv_w_in_2", "conv_w_2", "conv_w_out_2", "router_w_2", "moe_w_gate_2", "moe_w_up_2", "moe_w_down_2"]


def kernel(**inputs):
    import concourse.bacc as _bacc
    from concourse.bass_utils import run_bass_kernel_spmd as _run

    nc = _bacc.Bacc("TRN2", target_bir_lowering=False, num_devices=1)
    const_k, dft_n = constants()
    given = {name: np.ascontiguousarray(inputs[name]) for name in _INS}
    given["const_k"], given["dft_n"] = const_k, dft_n
    arrays, aps = {}, {}
    for name, a in given.items():
        arrays[f"in_{name}_dram"] = a
        aps[name] = nc.dram_tensor(f"in_{name}_dram", a.shape, mybir.dt.from_np(a.dtype), kind="ExternalInput").ap()
    out = nc.dram_tensor("out_0_dram", (1, N, D), F32, kind="ExternalOutput").ap()
    block_kernel(nc, aps, out)
    r = _run(nc, [arrays], core_ids=[0])
    return r.results[0]["out_0_dram"]
```

```python
from contextlib import ExitStack

import numpy as np

import concourse.bass as bass
from concourse import mybir

F32 = mybir.dt.float32
ALU = mybir.AluOpType
ACT = mybir.ActivationFunctionType
AX = mybir.AxisListType

P = 128
D = 1024
DT = D // P
N = 512
NT = N // P
NC = 256
CT = NC // P
NK = N + NC
SEGS = 8
SEG = 64
TAPS = 31
PAD = TAPS // 2
SEGP = SEG + 2 * PAD
HEADS = 6
HD = 64
QKW = HEADS * 2 * HD
E = 16
CAP = 2 * N // E
PAIRS = E // 2
EPS = 1e-6
POOL_CONV = (1, 3, 5)
CONV_ORDER = (0, 1, 2, 4, 3, 6, 5, 7)
N_VEC = 25
LAM_INIT = 0.2
RING = 6
BLK = DT * N

COL = {}
_at = 0
for _n, _w in (
    ("c", 8), ("c2", 8), ("cctx", 8), ("norm1_g", 8), ("norm2_g", 8), ("final_g", 8), ("b_pw1", 16), ("b_dw", 8),
    ("ln_g", 8), ("ln_b", 8), ("b_pw2", 8), ("mix_g", 16), ("ffn_g", 16),
    ("b_mod0", 48), ("b_mod1", 48), ("w_conv3", 24), ("q_g", 1), ("k_g", 1), ("subln", 1), ("to_next_row", 5),
    ("b_mod2", 48), ("w_dw", TAPS * 8),
):
    COL[_n] = _at
    _at += _w
VEC_ROWS = [128, 123, 128, 128, 40]

KCOL = {}
_at = 0
for _n, _w in (("ident", 128), ("ones_d", 128), ("ones_v", 128), ("ones_h", 128), ("rope", 128), ("dft_d", 256),
               ("cos", N), ("sin", N), ("iota", CAP)):
    KCOL[_n] = (_at, _w)
    _at += _w
KW = _at


def constants():
    k = np.zeros((P, KW), np.float32)

    def put(name, a):
        at, w = KCOL[name]
        k[:, at:at + w] = a

    put("ident", np.eye(P))
    put("ones_d", np.full((P, P), 1.0 / D))
    put("ones_v", np.full((P, P), 1.0 / P))
    put("ones_h", np.kron(np.eye(2), np.full((HD, HD), 1.0 / HD)))
    rope = np.zeros((HD, HD))
    for i in range(16):
        rope[16 + i, i] = rope[48 + i, 32 + i] = -1
        rope[i, 16 + i] = rope[32 + i, 48 + i] = 1
    put("rope", np.kron(np.eye(2), rope))
    d = np.arange(HD)
    ang = 2 * np.pi * (np.outer(d, d) % HD) / HD
    put("dft_d", np.hstack([np.kron(np.eye(2), f(ang) / 8.0) for f in (np.cos, np.sin)]))
    inv = (np.float32(10000.0) ** (-np.arange(16, dtype=np.float32) / np.float32(16))).astype(np.float32)
    row, col = np.arange(N) // 64, np.arange(N) % 64
    ar, ac = (np.outer(inv, t.astype(np.float32)).astype(np.float32) for t in (row, col))
    ang = np.vstack([ar, ar, ac, ac] * 2)
    put("cos", np.cos(ang.astype(np.float64)))
    put("sin", np.sin(ang.astype(np.float64)))
    put("iota", np.arange(1, CAP + 1)[None, :])
    t = np.arange(N)
    ang = 2 * np.pi * (np.outer(t, t) % N) / N
    dft_n = (np.vstack([np.cos(ang), -np.sin(ang)]) / np.sqrt(N)).astype(np.float32)
    return k, dft_n


def block_kernel(nc, A, out):
    def blk(w, r0, c0):
        return w[r0:r0 + D, c0:c0 + N].rearrange("(k p) n -> p k n", p=P)

    mods = [A["w_mod"][0], A["ada_w_2"][0], A["ada_w_2"][1]]
    stream = []
    owner_release = []

    tile_by = []

    def tiles(engines):
        t0 = len(tile_by)
        tile_by.extend(engines)
        return t0

    def add(src, release, slot=None):
        n = len(stream)
        stream.append((src, n % RING if slot is None else slot))
        owner_release.append(release)
        return n

    def add_mod(rnd):
        return [add(blk(mods[rnd // 3], 0, (rnd % 3) * 2048 + q * N), ("mod_row", rnd + 1)) for q in range(4)]

    T_X = tiles(["dve"] * 8)
    T_V = tiles(["dve"] * 2)
    B_MOD = {0: add_mod(0)}
    T_PW1 = tiles(["act"] * 16)
    B_PW1 = {}

    def add_pw1(b):
        last = T_PW1 + 8 * b + 8
        B_PW1[b] = (add(blk(A["conv_w_pw1"][0], 0, D + b * N), ("tile_done", last - 1)),
                    add(blk(A["conv_w_pw1"][0], 0, b * N), ("tile_done", last)))

    add_pw1(0)
    add_pw1(1)
    B_MOD[1] = add_mod(1)
    B_MOD[2] = add_mod(2)
    T_PW2 = tiles(["act"] * 8)
    B_PW2 = [add(blk(A["conv_w_pw2"][0], 0, b * N), ("tile_done", T_PW2 + 4 * b + 4)) for b in range(2)]
    T_W1, T_W2, B_W1, B_W2 = {}, {}, {}, {}
    for half in range(2):
        T_W1[half] = tiles(["act"] * 16)
        T_W2[half] = tiles(["dve"] * 8)
        B_W1[half], B_W2[half] = [], []
        for b in range(4):
            B_W1[half].append(add(blk(A["mlp_w1"][0], 0, half * 2048 + b * N), ("tile_done", T_W1[half] + 4 * b + 4)))
            if b < 3:
                B_MOD[3 + 3 * half + b] = add_mod(3 + 3 * half + b)
        for nh in range(2):
            for kq in range(2):
                B_W2[half].append(add(blk(A["mlp_w2"][0], half * 2048 + kq * D, nh * N),
                                      ("tile_done", T_W2[half] + 4 * nh + 4)))
    T_C = tiles(["act"] * 8)

    B_IN = []
    units = []
    IN_ORDER = [[("q", i) for i in range(4)],
                [("q", 4), ("q", 5), ("k", 0), ("k", 1), ("c", 0), ("c", 1)],
                [("k", i) for i in range(2, 6)] + [("c", i) for i in range(2, 6)],
                [("v", i) for i in range(NT + CT)],
                [("w", i) for i in range(NT + CT)] + [("f", 0), ("f", 1)]]
    in_tiles = []
    for b, order in enumerate(IN_ORDER):
        for kind, i in order:
            t = tiles(["dve" if kind == "f" else "act"])
            in_tiles.append((b, kind, i, t))
            if kind in "qkc":
                units.append((kind, i, t))
        B_IN.append(add(blk(A["attn_w_in_2"][0], 0, b * N), ("tile_done", t + 1), 4 + b % 2))
    T_F1 = tiles(["dve"] * 4)
    T_F2 = tiles(["dve"] * 2)
    B_CS = add(blk(A["dft_n"], 0, 0), ("tile_done", T_F2 + 2), 5)
    T_WO = tiles(["dve"] * 8)
    B_WO = [add(blk(A["attn_w_out_2"][0], 0, b * N), ("tile_done", T_WO + 4 * b + 4), 4 + b) for b in range(2)]
    FIRST = len(stream)
    assert FIRST % RING == 0
    T_O = {}
    order_o = []
    T_LOG, T_LT, T_H, T_AFF, T_POS = {}, {}, {}, {}, {}

    def add_route(layer):
        T_LOG[layer] = tiles(["dve"])
        T_H[layer] = [tiles(["act"])]
        T_LT[layer] = tiles(["dve"])
        T_H[layer] += [tiles(["act"]) for m in range(1, 4)]
        T_AFF[layer] = tiles(["dve"])
        T_H[layer] += [tiles(["act"]) for m in range(4, 8)]
        T_POS[layer] = tiles(["dve"])

    add_route(0)
    for half in range(2):
        for j in range(4 * half, 4 * half + 4):
            T_O[j] = tiles(["act", "dve", "dve"])
    for half in range(2):
        last = T_O[4 * half + 3]
        for pos, part in enumerate((1, 2, 0)):
            order_o.append((part, half))
            add(blk(A["conv_w_in_2"][0], 0, part * D + half * N), ("tile_done", last + pos + 1))
    T_OO = tiles(["dve"] * 8)
    for b in range(2):
        add(blk(A["conv_w_out_2"][0], 0, b * N), ("tile_done", T_OO + 4 * b + 4))
    add_route(1)
    T_OUT = tiles(["dve"] * 8)
    SECOND = len(stream)
    MOE_BLOCKS = 12 * PAIRS
    loads = [0] * RING
    landed_at = []
    prev = [None] * RING
    prev_of = []
    MOE_LOADS = {}
    for n, (src, slot) in enumerate(stream):
        if n == FIRST:
            MOE_LOADS[0] = list(loads)
            loads = [x + MOE_BLOCKS // RING for x in loads]
        loads[slot] += 1
        landed_at.append((slot, 16 * loads[slot]))
        prev_of.append(prev[slot])
        prev[slot] = n
    MOE_LOADS[1] = list(loads)
    count = {"act": 0, "dve": 0}
    tile_free = []
    for e in tile_by:
        count[e] += 1
        tile_free.append((e, count[e]))

    with ExitStack() as ctx:
        def sb(name, shape, dt=F32):
            return ctx.enter_context(nc.sbuf_tensor(name, shape, dt))

        S = {}

        def sem(name):
            S[name] = ctx.enter_context(nc.semaphore(name))
            return S[name]

        psum = ctx.enter_context(nc.psum_tensor("psum", [P, 8, 512], F32))
        STAT, MISC = 6, 7

        ring = sb("ring", [P, RING * BLK])
        xT = sb("xT", [P, DT, N])
        hT = sb("hT", [P, DT, N])
        arena = sb("arena", [P, 12288])
        K = sb("K", [P, KW])
        vecT = sb("vecT", [P, 5 * P])
        cpad = sb("cpad", [P, DT, 32])
        mod_rows = sb("mod_rows", [P, N])
        mod_raw = sb("mod_raw", [P, 9, 2, 16])
        modv = sb("modv", [P, 4, 48])
        gain = sb("gain", [P, 8, DT])
        gain1 = sb("gain1", [P, DT])
        sq = sb("sq", [P, 2, N])
        rms = sb("rms", [P, N])
        rstd = sb("rstd", [P, N])
        tmp = sb("tmp", [P, 2, N])
        eps = sb("eps", [P, 1])
        one = sb("one", [P, 1])
        gqk = sb("gqk", [P, 3])
        lam_in = sb("lam_in", [P, 4, HD])
        lam_pr = sb("lam_pr", [P, HD])
        lam = sb("lam", [P, 6])
        rw = sb("rw", [P, 2, DT, E])
        small = sb("small", [P, 32])
        logits = sb("logits", [P, NT, E])
        aff = sb("aff", [P, NT, E])
        pos = sb("pos", [P, NT, E])
        top8 = sb("top8", [E, 8])

        def const(name):
            at, w = KCOL[name]
            return K[:, at:at + w]

        ident, cos, sin = const("ident"), const("cos"), const("sin")

        def slot_ap(slot):
            return ring[:, slot * BLK:(slot + 1) * BLK].rearrange("p (k n) -> p k n", k=DT)

        def carve(base, at, *shape):
            n = int(np.prod(shape))
            v = base[:, at:at + n]
            if len(shape) == 2:
                v = v.rearrange("p (a b) -> p a b", a=shape[0])
            if len(shape) == 3:
                v = v.rearrange("p (a b c) -> p a b c", a=shape[0], b=shape[1])
            return v

        vec_rows = carve(arena, DT * SEGS * SEGP, 5, P)
        x_tok = hT[:, :, :].rearrange("p a b -> p (a b)").rearrange("p (t d) -> p t d", t=NT)
        upad = carve(arena, 0, DT, SEGS, SEGP)
        cv = carve(arena, DT * SEGS * SEGP, DT, N)
        glu_a = carve(arena, 10112, 2, N)
        glu_s = carve(arena, 11136, 2, N)
        hid = carve(arena, 0, 16, N)
        ctx_tok = carve(arena, 8192, CT, D)
        xcT = carve(arena, 10240, DT, NC)
        qT = carve(ring, 0, HEADS, N)
        kT = carve(ring, HEADS * N, HEADS, NK)
        vtok = carve(ring, 2 * BLK, NT + CT, QKW)
        fT = carve(ring, 2 * BLK + 4608, 2, N)
        hcT = carve(ring, 2 * BLK + 5632, DT, NC)
        qs = carve(arena, 0, 4, N)
        t_cos = carve(arena, 2048, 2, N)
        t_sin = carve(arena, 3072, 2, N)
        dft1 = carve(arena, 4096, NT, 512)
        prob = carve(arena, 0, 4, NK)
        attn = carve(arena, 3072, 2, NK)
        aT = carve(arena, 4608, HEADS, N)
        o_sb = carve(arena, 7680, N)
        prob1 = carve(arena, 8192, NK)
        cg = carve(arena, 0, 2, N)
        zpad = carve(arena, 1024, N + 2)
        zc = carve(arena, 1540, N)
        mixed = carve(arena, 2052, DT, N)
        h_tok = carve(arena, 0, NT, D)
        xsT = carve(arena, 4096, DT, P)
        sel = carve(arena, 5120, NT, 2, CAP)
        gsel = carve(arena, 5632, NT, 2, CAP)
        gselT = carve(arena, 6144, N)
        sil = carve(arena, 6656, 2, N)
        act_e = carve(arena, 7680, 2, N)
        aeT = carve(arena, 8704, DT, P)
        y_sb = carve(arena, 9728, D)
        lgT, affT, left = (carve(arena, 10752 + N * m, N)[0:E, :] for m in range(3))
        out_tok = carve(arena, 0, NT, D)

        landed = [sem(f"landed{i}") for i in range(RING)]
        for name in (
            "vec_in", "x_in", "ctx_in", "const_in", "small_in", "stored",
            "tile_done", "act_free", "dve_free", "act_link", "dve_link", "pool_link", "pads_zero",
            "tap_ready", "tap_added", "c_silu", "mod_row", "mod_row_sb", "mod_turned", "mod_raw_ready", "mod_ready",
            "sq_ready", "sq_used", "rms_ready", "scaled", "h_ready",
            "u_ready", "conv_done", "mean_done", "mean_sb", "centered",
            "x_pw2", "x_moe", "gains", "hid_ready", "lam_sum", "lam_exp", "qk_in",
            "qk_stat", "qk_rms", "qk_normed", "qk_rot", "qk_done",
            "scores", "score_half", "neg_max", "probs", "attn_ready", "attn_turned", "aT_sb", "pv_done", "o_in", "o_stat", "o_rms",
            "o_ready",
            "soft_exp", "aff_ready", "pos_ready", "acc_zero",
            "sel_ready", "gsel_ready", "gathered", "xs_act", "xs_dve", "gselT_done", "gselT_sb",
            "gate_done", "up_done", "down_done", "sil_ready", "a_ready", "aT_done", "aT_act", "aT_dve",
            "y_act", "y_dve", "scattered", "acc_added",
        ):
            sem(name)
        FREE = {"act": S["act_free"], "dve": S["dve_free"]}

        def emptied(t0):
            return lambda j: (FREE[tile_free[t0 + j][0]], tile_free[t0 + j][1])

        def score_banks(b):
            return 3 * b

        def score_set(b):
            return psum[:, 3 * b:3 * b + 3, :].rearrange("p a b -> p (a b)").rearrange("p (c k) -> p c k", c=2)

        def arrived(eng, n):
            slot, value = landed_at[n]
            eng.wait_ge(landed[slot], value)
            return slot_ap(stream[n][1])

        NORM1, LN, NORM2, FINAL, MIX0, CTXN, FFN0, MIX1, FFN1 = range(9)
        BIASED = {NORM1: 0, LN: 1, NORM2: 2, MIX0: 3, CTXN: 4, FFN0: 5, MIX1: 6, FFN1: 7}

        block = ctx.enter_context(nc.Block())

        @block.sync
        def _(sp):
            def load(n):
                src, slot = stream[n]
                if prev_of[n] is not None:
                    name, value = owner_release[prev_of[n]]
                    sp.wait_ge(S[name], value)
                sp.dma_start(slot_ap(slot), src).then_inc(landed[slot], 16)

            def load_experts(layer):
                for s in range(RING):
                    own = [n for n in range(FIRST if layer == 0 else SECOND) if stream[n][1] == s][-1]
                    name, value = owner_release[own]
                    sp.wait_ge(S[name], value)
                if layer == 0:
                    sp.wait_ge(S["pv_done"], HEADS)
                s0 = 0 if layer == 0 else SECOND % RING
                gate, up, down = (A[f"moe_w_{x}_2"][layer].rearrange("e (k p) n -> e p k n", p=P)
                                  for x in ("gate", "up", "down"))
                with sp.Fori(0, PAIRS) as i:
                    n = i + PAIRS * layer
                    plan = [(gate, 0, "up_done", 2 * n + 1), (gate, 1, "down_done", 2 * n),
                            (up, 0, "down_done", 2 * n + 1), (up, 1, "gate_done", 2 * n + 1),
                            (down, 0, "gate_done", 2 * n + 2), (down, 1, "up_done", 2 * n + 2)]
                    for m, (w, half, name, value) in enumerate(plan):
                        sp.wait_ge(S[name], value)
                        for e in range(2):
                            slot = (s0 + 2 * m + e) % RING
                            src = w[bass.ds(2 * i + e, 1), :, :, half * N:(half + 1) * N]
                            sp.dma_start(slot_ap(slot), src.rearrange("e p k n -> p (e k) n"))\
                                .then_inc(landed[slot], 16)

            sp.dma_start(x_tok[:, :, :], A["x"][0].rearrange("(t p) d -> p t d", p=P)).then_inc(S["x_in"], 16)
            sp.dma_start(K[:, :], A["const_k"]).then_inc(S["const_in"], 16)
            sp.wait_ge(S["vec_in"], 16 * N_VEC)
            for n in range(FIRST):
                load(n)
            load_experts(0)
            for n in range(FIRST, SECOND):
                if prev_of[n] is not None and n < FIRST + RING:
                    sp.wait_ge(S["down_done"], 2 * PAIRS + 1)
                    src, slot = stream[n]
                    sp.dma_start(slot_ap(slot), src).then_inc(landed[slot], 16)
                else:
                    load(n)
            load_experts(1)
            for t in range(NT):
                sp.wait_ge(*emptied(T_OUT)(2 * t + 1))
                sp.dma_start(out[0, t * P:(t + 1) * P, :], out_tok[:, t, :]).then_inc(S["stored"], 16)
            sp.wait_ge(S["stored"], 16 * NT)

        @block.gpsimd
        def _(pool):
            link_n = [0]

            def link(ins):
                link_n[0] += 1
                ins.then_inc(S["pool_link"], 1)
                pool.wait_ge(S["pool_link"], link_n[0])

            pool.memset(cpad[:, :, :], 0.0).then_inc(S["pads_zero"], 1)
            pool.memset(eps[:, :], EPS).then_inc(S["pads_zero"], 1)
            pool.memset(one[:, :], 1.0).then_inc(S["pads_zero"], 1)
            pool.memset(upad[:, :, :, 0:PAD], 0.0).then_inc(S["pads_zero"], 1)
            pool.memset(upad[:, :, :, PAD + SEG:SEGP], 0.0).then_inc(S["pads_zero"], 1)

            def mod_bias(rnd):
                a, r = divmod(rnd, 3)
                pool.wait_ge(S["mod_raw_ready"], rnd + 1)
                bias = vecT[:, COL[f"b_mod{a}"] + 16 * r:COL[f"b_mod{a}"] + 16 * r + 16]
                slots = [[0], [1, 2], [3]][a]
                for m, v in enumerate(slots):
                    ins = pool.tensor_tensor(modv[:, v, 16 * r:16 * r + 16], mod_raw[:, rnd, m, :], bias, ALU.add)
                    if v == slots[-1]:
                        ins.then_inc(S["mod_ready"], 1)
                    else:
                        link(ins)
                pool.wait_ge(S["mod_ready"], rnd + 1)

            made = []

            def make_gain(n, v, part, g):
                if made:
                    pool.wait_ge(S["gains"], made[-1])
                link(pool.tensor_scalar(gain1[:, :], modv[:, v, part:part + 8], 1.0, None, ALU.add))
                made.append(len(made) + 1)
                pool.tensor_tensor(gain[:, n, :], gain1[:, :], vecT[:, COL[g[0]] + g[1]:COL[g[0]] + g[1] + 8],
                                   ALU.mult).then_inc(S["gains"], 1)

            mod_bias(0)
            make_gain(0, 0, 8, ("norm1_g", 0))
            for m, j in enumerate(POOL_CONV):
                for k in range(TAPS):
                    g = TAPS * m + k
                    pool.wait_ge(S["tap_ready"], g + 1)
                    if k == 0:
                        pool.tensor_copy(cv[:, j, :], sq[:, g % 2, :]).then_inc(S["tap_added"], 1)
                    else:
                        pool.wait_ge(S["tap_added"], g)
                        pool.tensor_tensor(cv[:, j, :], cv[:, j, :], sq[:, g % 2, :], ALU.add)\
                            .then_inc(S["tap_added"], 1)
            mod_bias(1)
            mod_bias(2)
            made.append(len(made) + 1)
            pool.tensor_tensor(gain[:, 7, :], modv[:, 0, 16:24], vecT[:, COL["b_pw2"]:COL["b_pw2"] + 8], ALU.mult)\
                .then_inc(S["gains"], 1)
            make_gain(1, 0, 32, ("norm2_g", 0))
            for rnd in range(3, 9):
                mod_bias(rnd)
                if rnd == 5:
                    make_gain(2, 1, 8, ("mix_g", 0))
                    make_gain(3, 2, 8, ("mix_g", 0))
                    make_gain(4, 1, 32, ("ffn_g", 0))
            make_gain(5, 3, 8, ("mix_g", 8))
            make_gain(6, 3, 32, ("ffn_g", 8))
            for layer in range(2):
                pool.wait_ge(*emptied(T_H[layer][7])(0))
                pool.memset(hT[:, :, :], 0.0).then_inc(S["acc_zero"], 1)

        @block.scalar
        def _(act):
            g0 = [("c", 0), ("c_2", 8), ("norm2_g", 32), ("norm1_g", 24), ("conv_b_pw1", 48), ("conv_b_dw", 64),
                  ("conv_ln_g", 72), ("conv_ln_b", 80), ("conv_b_pw2", 88)]
            n_vec = 0

            def rows(dst, src):
                nonlocal n_vec
                act.dma_start(dst, src).then_inc(S["vec_in"], 16)
                n_vec += 1

            for name, at in g0:
                w = A[name].shape[1] // P
                rows(vec_rows[at:at + w, 0, :], A[name][0].rearrange("(r p) -> r p", p=P))
            for name, at in (("c_ctx_2", 16), ("final_g", 40)):
                rows(vec_rows[at:at + 8, 0, :], A[name].rearrange("(r p) -> r p", p=P))
            for name, at in (("norm_mix_2", 96), ("norm_ffn_2", 112)):
                rows(vec_rows[at:at + 16, 0, :], A[name].rearrange("l (r p) -> (l r) p", p=P))
            rows(vec_rows[0:48, 1, :], A["b_mod"][0].rearrange("(r p) -> r p", p=P))
            rows(vec_rows[48:96, 1, :], A["ada_b_2"][0].rearrange("(r p) -> r p", p=P))
            rows(vec_rows[96:120, 1, :], A["conv_w_2"][0].rearrange("k (r p) -> (k r) p", p=P))
            for m, name in enumerate(("attn_q_norm_2", "attn_k_norm_2")):
                for half in range(2):
                    rows(vec_rows[120 + m:121 + m, 1, half * HD:(half + 1) * HD], A[name])
            rows(vec_rows[122:123, 1, :], A["attn_subln_2"])
            rows(vec_rows[0:48, 2, :], A["ada_b_2"][1].rearrange("(r p) -> r p", p=P))
            taps = A["conv_w_dw"][0].rearrange("k (r p) -> (k r) p", p=P)
            rows(vec_rows[48:128, 2, :], taps[0:80])
            rows(vec_rows[0:128, 3, :], taps[80:208])
            rows(vec_rows[0:40, 4, :], taps[208:248])
            assert n_vec == N_VEC
            for m, name in enumerate(("lam_q1_2", "lam_k1_2", "lam_q2_2", "lam_k2_2")):
                act.dma_start(lam_in[:, m, :], A[name][0].partition_broadcast(P)).then_inc(S["small_in"], 16)
            for layer in range(2):
                act.dma_start(rw[:, layer, :, :], A["router_w_2"][layer].rearrange("(k p) e -> p k e", p=P))\
                    .then_inc(S["small_in"], 16)

            link_n = [0]

            def link(ins):
                link_n[0] += 1
                ins.then_inc(S["act_link"], 1)
                act.wait_ge(S["act_link"], link_n[0])

            def squares(n, src, ready, width=N, js=range(DT)):
                for j in js:
                    g = DT * n + j
                    act.wait_ge(*ready(j))
                    if g >= 2:
                        act.wait_ge(S["sq_used"], g - 1)
                    act.activation(sq[:, g % 2, 0:width], src[:, j, :], ACT.Square).then_inc(S["sq_ready"], 1)

            def root(n, width=N):
                act.wait_ge(S["sq_used"], DT * n + DT)
                if n:
                    act.wait_ge(S["scaled"], DT * n)
                act.activation(rms[:, 0:width], psum[:, STAT, 0:width], ACT.Sqrt, bias=eps[:, 0:1])\
                    .then_inc(S["rms_ready"], 1)

            def shift(n, dst, bias, func=ACT.Identity):
                for j in range(DT):
                    act.wait_ge(S["scaled"], DT * n + j + 1)
                    act.activation(dst[:, j, :], dst[:, j, :], func, bias=bias[:, j:j + 1]).then_inc(S["h_ready"], 1)

            def mod_row(rnd):
                act.wait_ge(S["mod_row"], rnd + 1)
                act.activation(mod_rows[:, :], psum[:, MISC, :], ACT.Copy).then_inc(S["mod_row_sb"], 1)

            def mod_turned(rnd):
                act.wait_ge(S["mod_turned"], rnd + 1)
                picks = [[0], [1, 2], [1]][rnd // 3]
                view = psum[:, MISC, :].rearrange("p (j q c) -> p q j c", j=4, q=4)
                for m, c in enumerate(picks):
                    act.activation(mod_raw[:, rnd, m, :].rearrange("p (q j) -> p q j", q=4), view[:, :, :, c], ACT.Copy)\
                        .then_inc(S["mod_raw_ready" if m == len(picks) - 1 else "act_link"], 1)
                    if m < len(picks) - 1:
                        link_n[0] += 1
                        act.wait_ge(S["act_link"], link_n[0])

            act.sem_inc(S["y_act"], 1)
            act.wait_ge(FREE["dve"], T_V + 2)
            act.wait_ge(S["pads_zero"], 5)
            act.activation(cpad[:, :, 0:3], vecT[:, 0:24].rearrange("p (i k) -> p k i", i=3), ACT.Silu)\
                .then_inc(S["c_silu"], 1)
            squares(NORM1, xT, emptied(T_X))
            root(NORM1)
            mod_row(0)
            mod_turned(0)
            act.wait_ge(S["mod_ready"], 1)
            shift(NORM1, hT, modv[:, 0, 0:8])

            def pw1(j):
                for m, dst in enumerate((glu_s, glu_a)):
                    t = T_PW1 + 2 * j + m
                    act.wait_ge(S["tile_done"], t + 1)
                    if j >= 2:
                        act.wait_ge(S["u_ready"], j - 1)
                    col = COL["b_pw1"] + (8 if m == 0 else 0) + j
                    act.activation(dst[:, j % 2, :], psum[:, t % 6, :], ACT.Sigmoid if m == 0 else ACT.Identity,
                                   bias=vecT[:, col:col + 1]).then_inc(FREE["act"], 1)

            pw1(0)
            pw1(1)
            between = {9: [(pw1, 2)], 20: [(pw1, 3)], 31: [(pw1, 4)], 42: [(pw1, 5)], 53: [(pw1, 6)], 64: [(pw1, 7)],
                       76: [(mod_row, 1), (mod_turned, 1)]}
            for m, j in enumerate(POOL_CONV):
                for k in range(TAPS):
                    g = TAPS * m + k
                    for step, arg in between.get(g, ()):
                        step(arg)
                    if k == 0:
                        act.wait_ge(S["u_ready"], j + 1)
                    if g >= 2:
                        act.wait_ge(S["tap_added"], g - 1)
                    elif g == 0:
                        act.wait_ge(S["sq_used"], DT)
                    dst = sq[:, g % 2, :].rearrange("p (s w) -> p s w", s=SEGS)
                    w = vecT[:, COL["w_dw"] + k * 8 + j:COL["w_dw"] + k * 8 + j + 1]
                    u = upad[:, j, :, k:k + SEG]
                    if k == 0:
                        act.activation(dst, u, ACT.Identity, scale=w,
                                       bias=vecT[:, COL["b_dw"] + j:COL["b_dw"] + j + 1]).then_inc(S["tap_ready"], 1)
                    else:
                        act.activation(dst, u, ACT.Copy, scale=w).then_inc(S["tap_ready"], 1)
            mod_row(2)
            mod_turned(2)
            act.wait_ge(S["mean_done"], 1)
            act.activation(tmp[:, 0, :], psum[:, STAT, :], ACT.Copy).then_inc(S["mean_sb"], 1)
            squares(LN, cv, lambda j: (S["centered"], j + 1))
            root(LN)
            shift(LN, hT, vecT[:, COL["ln_b"]:COL["ln_b"] + 8], ACT.Silu)
            act.wait_ge(S["gains"], 2)
            for j in range(DT):
                t = T_PW2 + j
                act.wait_ge(S["tile_done"], t + 1)
                if j >= 2:
                    act.wait_ge(S["x_pw2"], j - 1)
                act.activation(tmp[:, j % 2, :], psum[:, t % 6, :], ACT.Identity, bias=gain[:, 7, j:j + 1],
                               scale=modv[:, 0, 16 + j:17 + j]).then_inc(FREE["act"], 1)
                squares(NORM2, xT, lambda j: (S["x_pw2"], j + 1), js=[j])
            root(NORM2)
            shift(NORM2, hT, modv[:, 0, 24:32])
            act.dma_start(ctx_tok[:, :, :], A["ctx_2"][0].rearrange("(t p) d -> p t d", p=P))\
                .then_inc(S["ctx_in"], 16)
            for half in range(2):
                for m in range(16):
                    t = T_W1[half] + m
                    act.wait_ge(S["tile_done"], t + 1)
                    act.activation(hid[:, m, :], psum[:, t % 6, :], ACT.Relu).then_inc(FREE["act"], 1)
                    if m in (3, 7, 11):
                        mod_row(3 + 3 * half + m // 4)
                    if m in (4, 8, 12):
                        mod_turned(3 + 3 * half + m // 4 - 1)
            squares(FINAL, xT, emptied(T_W2[1]))
            root(FINAL)
            for j in range(DT):
                act.wait_ge(S["tile_done"], T_C + j + 1)
                act.activation(xcT[:, j, :], psum[:, (T_C + j) % 6, 0:NC], ACT.Copy).then_inc(FREE["act"], 1)
            squares(MIX0, xT, lambda j: (S["scaled"], DT * FINAL + j + 1))
            root(MIX0)
            squares(CTXN, xcT, emptied(T_C), NC)
            shift(MIX0, hT, modv[:, 1, 0:8])
            root(CTXN, NC)
            shift(CTXN, hcT, modv[:, 2, 0:8])

            act.wait_ge(S["lam_sum"], 2)
            act.activation(lam[:, 2:4], lam[:, 0:2], ACT.Exp).then_inc(S["lam_exp"], 1)

            def unit_in(u):
                kind, i, t = units[u]
                w = NC if kind == "c" else N
                act.wait_ge(S["tile_done"], t + 1)
                if u >= 4:
                    act.wait_ge(S["qk_done"], u - 3)
                if u >= 2:
                    act.wait_ge(S["qk_stat"], u - 1)
                act.activation(qs[:, u % 4, 0:w], psum[:, t % 6, 0:w], ACT.Copy).then_inc(S["qk_in"], 1)
                act.activation(sq[:, u % 2, 0:w], psum[:, t % 6, 0:w], ACT.Square).then_inc(FREE["act"], 1)

            def unit_root(u):
                w = NC if units[u][0] == "c" else N
                act.wait_ge(S["qk_stat"], u + 1)
                if u:
                    act.wait_ge(S["qk_normed"], u)
                act.activation(rms[:, 0:w], psum[:, STAT, 0:w], ACT.Sqrt, bias=eps[:, 0:1]).then_inc(S["qk_rms"], 1)

            u = 0
            for b, kind, i, t in in_tiles:
                if kind in "qkc":
                    unit_in(u)
                    if u:
                        unit_root(u - 1)
                    u += 1
                elif kind in "vw":
                    if u == len(units):
                        unit_root(u - 1)
                        u += 1
                    act.wait_ge(S["tile_done"], t + 1)
                    if kind == "v":
                        dst, src = vtok[:, i, 0:N], psum[:, t % 6, :]
                    else:
                        dst, src = vtok[:, i, N:QKW], psum[:, t % 6, 0:QKW - N]
                    act.activation(dst, src, ACT.Copy).then_inc(FREE["act"], 1)

            def exps(it):
                b = it % 2
                if it >= 2:
                    act.wait_ge(S["attn_ready"], it - 1)
                act.wait_ge(S["neg_max"], it + 1)
                for m in range(2):
                    act.activation(prob[:, 2 * b + m, :], score_set(b)[:, m, :], ACT.Exp,
                                   bias=small[:, 28 + 2 * b + m:29 + 2 * b + m],
                                   accum_out=small[:, 4 + 2 * b + m:5 + 2 * b + m]).then_inc(S["probs"], 1)

            def turn_in(it):
                act.wait_ge(S["attn_turned"], it + 1)
                m = it % 4
                if m == 0 and it:
                    act.wait_ge(S["pv_done"], it // 4)
                act.activation(aT[:, 0:4, m * P:(m + 1) * P], psum[:, 6, :].rearrange("p (a b) -> p a b", a=4),
                               ACT.Copy).then_inc(S["aT_sb"], 1)
                act.activation(aT[:, 4:6, m * P:(m + 1) * P], psum[:, 7, 0:256].rearrange("p (a b) -> p a b", a=2),
                               ACT.Copy).then_inc(S["aT_sb"], 1)

            def head_out(h):
                act.wait_ge(S["pv_done"], h + 1)
                if h:
                    act.wait_ge(S["o_ready"], h)
                act.activation(o_sb, psum[:, 7, :], ACT.Copy).then_inc(S["o_in"], 1)
                act.activation(sq[:, 0, :], psum[:, 7, :], ACT.Square).then_inc(S["o_in"], 1)

            def head_root(h):
                act.wait_ge(S["o_stat"], h + 1)
                act.activation(rms[:, :], psum[:, 6, :], ACT.Sqrt, bias=eps[:, 0:1]).then_inc(S["o_rms"], 1)

            exps(0)
            for it in range(4 * HEADS):
                if it + 1 < 4 * HEADS:
                    exps(it + 1)
                if it and it % 4 == 0:
                    head_out(it // 4 - 1)
                if it > 4 and it % 4 == 1:
                    head_root(it // 4 - 1)
                turn_in(it)
            head_out(HEADS - 1)
            head_root(HEADS - 1)

            squares(FFN0, xT, emptied(T_WO))
            root(FFN0)
            shift(FFN0, hT, modv[:, 1, 24:32])

            def softmax(layer):
                for m, t in enumerate(T_H[layer]):
                    if m == 1:
                        act.wait_ge(*emptied(T_LT[layer])(0))
                        act.activation(aff[:, :, :], logits[:, :, :], ACT.Exp).then_inc(S["soft_exp"], 1)
                    tt, half = divmod(m, 2)
                    act.wait_ge(S["tile_done"], t + 1)
                    act.activation(h_tok[:, tt, half * N:(half + 1) * N], psum[:, t % 6, :], ACT.Copy)\
                        .then_inc(FREE["act"], 1)

            def experts(layer):
                with act.Fori(0, PAIRS) as i:
                    n = i + PAIRS * layer
                    act.wait_ge(S["gathered"], 2 * n + 1)
                    act.activation(xsT[:, 0:4, :], psum[:, 6, :].rearrange("p (a b) -> p a b", a=4), ACT.Copy)\
                        .then_inc(S["xs_act"], 1)
                    act.wait_ge(S["gate_done"], 2 * n + 1)
                    act.wait_ge(S["a_ready"], 2 * n + 1)
                    act.activation(sil[:, 0, :], psum[:, 0, :], ACT.Silu).then_inc(S["sil_ready"], 1)
                    act.wait_ge(S["gselT_done"], n + 2)
                    act.activation(gselT, psum[:, 6, :], ACT.Copy).then_inc(S["gselT_sb"], 1)
                    act.wait_ge(S["gate_done"], 2 * n + 2)
                    act.activation(sil[:, 1, :], psum[:, 1, :], ACT.Silu).then_inc(S["sil_ready"], 1)
                    act.wait_ge(S["aT_done"], 2 * n + 1)
                    act.activation(aeT[:, 0:4, :], psum[:, 6, :].rearrange("p (a b) -> p a b", a=4), ACT.Copy)\
                        .then_inc(S["aT_act"], 1)
                    act.wait_ge(S["down_done"], 2 * n + 2)
                    act.activation(y_sb[:, 0:N], psum[:, 4, :], ACT.Copy).then_inc(S["y_act"], 1)

            softmax(0)
            experts(0)
            squares(MIX1, xT, lambda j: (S["x_moe"], j + 1))
            root(MIX1)
            act.wait_ge(S["mod_ready"], 9)
            shift(MIX1, hT, modv[:, 3, 0:8])
            for j in range(DT):
                t = T_O[j]
                act.wait_ge(S["tile_done"], t + 1)
                if j >= 2:
                    act.wait_ge(*emptied(T_O[j - 2] + 1)(0))
                act.activation(cg[:, j % 2, :], psum[:, t % 6, :], ACT.Copy).then_inc(FREE["act"], 1)
            squares(FFN1, xT, emptied(T_OO))
            root(FFN1)
            shift(FFN1, hT, modv[:, 3, 24:32])
            softmax(1)
            experts(1)

        @block.tensor
        def _(pe):
            def begin(t):
                if t >= 6:
                    e, v = tile_free[t - 6]
                    pe.wait_ge(FREE[e], v)
                return psum[:, t % 6, :]

            def dense(t, w, col, src, kts, width=N, start=True, stop=True, ready=None):
                bank = psum[:, t % 6, :]
                for k in range(kts):
                    if ready is not None:
                        pe.wait_ge(*(ready(k) if callable(ready) else (S[ready[0]], ready[1] + k + 1)))
                    ins = pe.matmul(bank[:, 0:width], w[:, k, col:col + P], src(k), start=start and k == 0,
                                    stop=stop and k == kts - 1)
                return ins

            def turn_tile(t, parts, ready=None):
                bank = begin(t)
                if ready is not None:
                    pe.wait_ge(*ready)
                for m, (src, p) in enumerate(parts):
                    w = src.shape[-1]
                    ins = pe.transpose(bank[0:w, m * P:m * P + p], src, ident[0:p, 0:p])
                ins.then_inc(S["tile_done"], 1)

            def norm_stat(n, width=N, js=range(DT)):
                for j in js:
                    if n and j == 0:
                        pe.wait_ge(S["rms_ready"], n)
                    g = DT * n + j
                    pe.wait_ge(S["sq_ready"], g + 1)
                    ins = pe.matmul(psum[:, STAT, 0:width], const("ones_d"), sq[:, g % 2, 0:width], start=j == 0,
                                    stop=j == DT - 1)
                    ins.then_inc(S["sq_used"], 1)

            def mod_gemv(rnd):
                ws = [arrived(pe, n) for n in B_MOD[rnd]]
                if rnd == 0:
                    pe.wait_ge(S["c_silu"], 1)
                else:
                    pe.wait_ge(S["mod_raw_ready"], rnd)
                for k in range(DT):
                    for q in range(4):
                        ins = pe.matmul(psum[32 * q:32 * q + 32, MISC, :], cpad[:, k, :], ws[q][:, k, :],
                                        start=k == 0, stop=k == DT - 1, skip_group_check=True)
                ins.then_inc(S["mod_row"], 1)

            def mod_turn(rnd):
                pe.wait_ge(S["mod_row_sb"], rnd + 1)
                for j in range(4):
                    ins = pe.transpose(psum[:, MISC, j * P:(j + 1) * P], mod_rows[:, j * P:(j + 1) * P], ident)
                ins.then_inc(S["mod_turned"], 1)

            for name in ("up_done", "down_done", "gselT_done"):
                pe.sem_inc(S[name], 1)
            pe.wait_ge(S["const_in"], 16)
            pe.wait_ge(S["x_in"], 16)
            for j in range(DT):
                turn_tile(T_X + j, [(x_tok[:, t, j * P:(j + 1) * P], P) for t in range(NT)])
            pe.wait_ge(S["vec_in"], 16 * N_VEC)
            turn_tile(T_V, [(vec_rows[0:VEC_ROWS[g], g, :], VEC_ROWS[g]) for g in range(4)])
            turn_tile(T_V + 1, [(vec_rows[0:VEC_ROWS[4], 4, :], VEC_ROWS[4])])
            norm_stat(NORM1)
            mod_gemv(0)
            mod_turn(0)

            def pw1(j):
                ws = B_PW1[j // 4]
                for m in range(2):
                    t = T_PW1 + 2 * j + m
                    begin(t)
                    w = arrived(pe, ws[m])
                    dense(t, w, (j % 4) * P, lambda k: hT[:, k, :], DT,
                          ready=("h_ready", 0) if j == 0 and m == 0 else None).then_inc(S["tile_done"], 1)

            for j in range(DT):
                pw1(j)
            for rnd in (1, 2):
                mod_gemv(rnd)
                mod_turn(rnd)
            pe.wait_ge(S["rms_ready"], 1)
            n_dve = n_pool = 0
            for m, j in enumerate(CONV_ORDER):
                if j in POOL_CONV:
                    n_pool += 1
                    pe.wait_ge(S["tap_added"], TAPS * n_pool)
                else:
                    n_dve += 1
                    pe.wait_ge(S["conv_done"], n_dve)
                ins = pe.matmul(psum[:, STAT, :], const("ones_d"), cv[:, j, :], start=m == 0, stop=m == DT - 1)
            ins.then_inc(S["mean_done"], 1)
            pe.wait_ge(S["mean_sb"], 1)
            norm_stat(LN)
            for j in range(DT):
                t = T_PW2 + j
                begin(t)
                w = arrived(pe, B_PW2[j // 4])
                dense(t, w, (j % 4) * P, lambda k: hT[:, k, :], DT,
                      ready=("h_ready", 8) if j == 0 else None).then_inc(S["tile_done"], 1)
                norm_stat(NORM2, js=[j - 1] if j else [])
            norm_stat(NORM2, js=[DT - 1])
            for half in range(2):
                for m in range(16):
                    t = T_W1[half] + m
                    begin(t)
                    w = arrived(pe, B_W1[half][m // 4])
                    dense(t, w, (m % 4) * P, lambda k: hT[:, k, :], DT,
                          ready=("h_ready", 16) if (half, m) == (0, 0) else None).then_inc(S["tile_done"], 1)
                    if m in (3, 7, 11):
                        mod_gemv(3 + 3 * half + m // 4)
                    if m in (4, 8, 12):
                        mod_turn(3 + 3 * half + m // 4 - 1)
                for nh in range(2):
                    for kq in range(2):
                        w = arrived(pe, B_W2[half][2 * nh + kq])
                        for j in range(4):
                            t = T_W2[half] + 4 * nh + j
                            if kq == 0:
                                begin(t)
                            ins = dense(t, w, j * P, lambda k: hid[:, 8 * kq + k, :], DT, start=kq == 0, stop=kq == 1,
                                        ready=("hid_ready", 16 * half + 8 * kq) if nh == 0 and j == 0 else None)
                            if kq == 1:
                                ins.then_inc(S["tile_done"], 1)
                                norm_stat(FINAL, js=[4 * nh + j - 1] if half == 1 and nh + j else [])
            norm_stat(FINAL, js=[DT - 1])
            pe.wait_ge(S["ctx_in"], 16)
            for j in range(DT):
                turn_tile(T_C + j, [(ctx_tok[:, t, j * P:(j + 1) * P], P) for t in range(CT)])
            norm_stat(MIX0)
            norm_stat(CTXN, NC)

            def unit_stat(u):
                w = NC if units[u][0] == "c" else N
                pe.wait_ge(FREE["act"], tile_free[units[u][2]][1])
                if u:
                    pe.wait_ge(S["qk_rms"], u)
                else:
                    pe.wait_ge(S["rms_ready"], CTXN + 1)
                pe.matmul(psum[:, STAT, 0:w], const("ones_h"), sq[:, u % 2, 0:w], start=True, stop=True)\
                    .then_inc(S["qk_stat"], 1)

            rotated = [0]

            def unit_rotate(u):
                if units[u][0] == "c":
                    return
                pe.wait_ge(S["qk_normed"], u + 1)
                if rotated[0]:
                    last = [v for v in range(u) if units[v][0] != "c"][-1]
                    pe.wait_ge(S["qk_done"], last + 1)
                rotated[0] += 1
                pe.matmul(psum[:, MISC, :], const("rope"), qs[:, u % 4, :], start=True, stop=True)\
                    .then_inc(S["qk_rot"], 1)

            u = 0
            first = True
            for b, kind, i, t in in_tiles:
                begin(t)
                w = arrived(pe, B_IN[b])
                if kind in "qkf":
                    col = {"q": i * P, "k": QKW + i * P, "f": 2 * QKW + QKW + i * P}[kind] - b * N
                    ins = dense(t, w, col, lambda k: hT[:, k, :], DT, ready=("h_ready", 8 * BIASED[MIX0]) if first else None)
                    first = False
                elif kind == "c":
                    pe.wait_ge(S["h_ready"], 8 * BIASED[CTXN] + 8)
                    ins = dense(t, w, QKW + i * P - b * N, lambda k: hcT[:, k, :], DT, width=NC)
                else:
                    width = N if kind == "v" else QKW - N
                    for k in range(DT):
                        src = hT[:, k, i * P:(i + 1) * P] if i < NT else hcT[:, k, (i - NT) * P:(i - NT + 1) * P]
                        ins = pe.matmul(psum[:, t % 6, 0:width], src, w[:, k, 0:width], start=k == 0, stop=k == DT - 1)
                ins.then_inc(S["tile_done"], 1)
                if kind in "qkc":
                    if u >= 1:
                        unit_stat(u - 1)
                    if u >= 2:
                        unit_rotate(u - 2)
                    u += 1
                elif kind == "v" and i < 2:
                    if i == 0:
                        unit_stat(u - 1)
                        unit_rotate(u - 2)
                    else:
                        unit_rotate(u - 1)
            for t in range(NT):
                begin(T_F1 + t)
                pe.wait_ge(*emptied(in_tiles[-1][3])(0))
                for ft in range(2):
                    ins = pe.matmul(psum[:, (T_F1 + t) % 6, 256 * ft:256 * ft + 256], fT[:, ft, t * P:(t + 1) * P],
                                    const("dft_d"), start=ft == 0, stop=ft == 1, skip_group_check=True)
                ins.then_inc(S["tile_done"], 1)
            w = arrived(pe, B_CS)
            for ft in range(2):
                begin(T_F2 + ft)
                pe.wait_ge(*emptied(T_F1)(3))
                for m in range(2 * NT):
                    t, part = m % NT, m // NT
                    ins = pe.matmul(psum[:, (T_F2 + ft) % 6, :], dft1[:, t, 256 * ft + P * part:256 * ft + P * part + P],
                                    w[:, m, :], start=m == 0, stop=m == 2 * NT - 1)
                ins.then_inc(S["tile_done"], 1)

            for e in ("act", "dve"):
                pe.wait_ge(FREE[e], [v for x, v in tile_free[:T_F2 + 2] if x == e][-1])
            pe.wait_ge(S["qk_done"], len(units))

            def scores(it):
                h, m = divmod(it, 4)
                if it >= 2:
                    pe.wait_ge(S["probs"], 2 * it - 2)
                banks = score_banks(it % 2)
                for c, lo, hi, bank, at in ((0, N, NK, 1, 0), (1, 0, N, 2, 0), (0, 0, N, 0, 0), (1, N, NK, 1, 256)):
                    if at:
                        pe.wait_ge(S["score_half"], it + 1)
                    ins = pe.matmul(psum[:, banks + bank, at:at + hi - lo], qT[64 * c:64 * c + 64, h, m * P:(m + 1) * P],
                                    kT[64 * c:64 * c + 64, h, lo:hi], start=True, stop=True, skip_group_check=True)
                    if bank == 1:
                        ins.then_inc(S["scores" if at else "score_half"], 1)

            def attn_turn(it):
                pe.wait_ge(S["attn_ready"], it + 1)
                if it:
                    pe.wait_ge(S["aT_sb"], 2 * it)
                if it > 4 and it % 4 == 1:
                    pe.wait_ge(S["o_rms"], it // 4)
                for k in range(6):
                    if k == 4 and it and it % 4 == 0:
                        pe.wait_ge(S["o_in"], 2 * (it // 4))
                    ins = pe.transpose(psum[:, 6 + k // 4, (k % 4) * P:(k % 4 + 1) * P],
                                       attn[:, it % 2, k * P:(k + 1) * P], ident)
                ins.then_inc(S["attn_turned"], 1)

            def values(h):
                pe.wait_ge(S["aT_sb"], 8 * h + 8)
                for k in range(6):
                    ins = pe.matmul(psum[:, 7, :], vtok[:, k, h * P:(h + 1) * P], aT[:, k, :], start=k == 0,
                                    stop=k == 5)
                ins.then_inc(S["pv_done"], 1)

            def head_stat(h):
                pe.wait_ge(S["o_in"], 2 * h + 2)
                pe.wait_ge(S["aT_sb"], min(2 * (4 * h + 5), 8 * HEADS))
                pe.matmul(psum[:, 6, :], const("ones_v"), sq[:, 0, :], start=True, stop=True)\
                    .then_inc(S["o_stat"], 1)

            scores(0)
            scores(1)
            for it in range(4 * HEADS):
                if it + 2 < 4 * HEADS:
                    scores(it + 2)
                if it and it % 4 == 0:
                    values(it // 4 - 1)
                if it > 4 and it % 4 == 1:
                    head_stat(it // 4 - 1)
                attn_turn(it)
            values(HEADS - 1)
            head_stat(HEADS - 1)
            for j in range(DT):
                t = T_WO + j
                if j == 0:
                    pe.wait_ge(S["aT_sb"], 8 * HEADS)
                    pe.wait_ge(S["o_rms"], HEADS)
                    pe.wait_ge(S["o_ready"], HEADS)
                else:
                    begin(t)
                w = arrived(pe, B_WO[j // 4])
                dense(t, w, (j % 4) * P, lambda k: hT[:, k, :], DT).then_inc(S["tile_done"], 1)
                norm_stat(FFN0, js=[j - 1] if j else [])
            norm_stat(FFN0, js=[DT - 1])

            def route(layer):
                n = FFN0 if layer == 0 else FFN1
                t = T_LOG[layer]
                begin(t)
                for k in range(DT):
                    pe.wait_ge(S["h_ready"], 8 * BIASED[n] + k + 1)
                    ins = pe.matmul(psum[0:E, t % 6, :], rw[:, layer, k, :], hT[:, k, :], start=k == 0, stop=k == DT - 1)
                ins.then_inc(S["tile_done"], 1)
                for m in range(8):
                    if m == 1:
                        pe.wait_ge(*emptied(t)(0))
                        begin(T_LT[layer])
                        for tt in range(NT):
                            ins = pe.transpose(psum[:, T_LT[layer] % 6, tt * E:(tt + 1) * E],
                                               lgT[:, tt * P:(tt + 1) * P], ident[0:E, 0:E])
                        ins.then_inc(S["tile_done"], 1)
                    if m == 4:
                        turn_tile(T_AFF[layer], [(aff[:, tt, :], P) for tt in range(NT)],
                                  ready=(S["aff_ready"], layer + 1))
                    tt, half = divmod(m, 2)
                    turn_tile(T_H[layer][m], [(hT[:, 4 * half + j, tt * P:(tt + 1) * P], P) for j in range(4)])
                pe.wait_ge(S["pos_ready"], layer + 1)
                begin(T_POS[layer])
                for m in range(NT):
                    ins = pe.transpose(psum[:, T_POS[layer] % 6, m * E:(m + 1) * E], left[:, m * P:(m + 1) * P],
                                       ident[0:E, 0:E])
                ins.then_inc(S["tile_done"], 1)

            def experts(layer):
                s0 = 0 if layer == 0 else SECOND % RING
                t = T_POS[layer]
                for e in ("act", "dve"):
                    pe.wait_ge(FREE[e], [v for x, v in tile_free[:t + 1] if x == e][-1])
                with pe.Fori(0, PAIRS) as i:
                    n = i + PAIRS * layer

                    def pair(m):
                        got = []
                        for e in range(2):
                            slot = (s0 + 2 * m + e) % RING
                            before = MOE_LOADS[layer][slot]
                            pe.wait_ge(landed[slot], 32 * i + 16 * (before + (2 * m + e) // RING + 1))
                            got.append(slot_ap(slot))
                        return got

                    def products(bank, m, src, name):
                        wa, wb = pair(m)
                        for k in range(DT):
                            for e, w in enumerate((wa, wb)):
                                ins = pe.matmul(psum[64 * e:64 * e + 64, bank, :], src[:, k, 64 * e:64 * e + 64],
                                                w[:, k, :], start=k == 0, stop=k == DT - 1, skip_group_check=True)
                        ins.then_inc(S[name], 1)

                    pe.wait_ge(S["sel_ready"], n + 1)
                    pe.wait_ge(S["acc_added"], 8 * n + 1)
                    for fj in range(DT):
                        for tt in range(NT):
                            ins = pe.matmul(psum[:, 6 + fj // 4, (fj % 4) * P:(fj % 4 + 1) * P],
                                            h_tok[:, tt, fj * P:(fj + 1) * P],
                                            sel[:, tt, :, :].rearrange("p a b -> p (a b)"),
                                            start=tt == 0, stop=tt == NT - 1)
                        if fj % 4 == 3:
                            ins.then_inc(S["gathered"], 1)
                    pe.wait_ge(S["xs_act"], n + 1)
                    pe.wait_ge(S["xs_dve"], n + 1)
                    pe.wait_ge(S["a_ready"], 2 * n + 1)
                    products(0, 0, xsT, "gate_done")
                    pe.wait_ge(S["gsel_ready"], n + 1)
                    for tt in range(NT):
                        ins = pe.transpose(psum[:, 6, tt * P:(tt + 1) * P],
                                           gsel[:, tt, :, :].rearrange("p a b -> p (a b)"), ident)
                    ins.then_inc(S["gselT_done"], 1)
                    products(1, 1, xsT, "gate_done")
                    products(2, 2, xsT, "up_done")
                    products(3, 3, xsT, "up_done")
                    pe.wait_ge(S["gselT_sb"], n + 1)
                    for half in range(2):
                        pe.wait_ge(S["a_ready"], 2 * n + 2 + half)
                        for j in range(4):
                            ins = pe.transpose(psum[:, 6 + half, j * P:(j + 1) * P],
                                               act_e[:, half, j * P:(j + 1) * P], ident)
                        ins.then_inc(S["aT_done"], 1)
                    pe.wait_ge(S["aT_act"], n + 1)
                    pe.wait_ge(S["aT_dve"], n + 1)
                    pe.wait_ge(S["y_act"], n + 1)
                    pe.wait_ge(S["y_dve"], n + 1)
                    products(4, 4, aeT, "down_done")
                    products(5, 5, aeT, "down_done")
                    pe.wait_ge(S["y_act"], n + 2)
                    for fj in range(DT):
                        if fj >= 2:
                            pe.wait_ge(S["acc_added"], 8 * n + fj)
                        if fj == 4:
                            pe.wait_ge(S["y_dve"], n + 2)
                        pe.matmul(psum[:, 6 + fj % 2, :], y_sb[:, fj * P:(fj + 1) * P], gselT, start=True, stop=True)\
                            .then_inc(S["scattered"], 1)

            route(0)
            experts(0)
            norm_stat(MIX1)
            oo = FIRST

            def mixed_at(k):
                return emptied(T_O[k] + 2)(0)

            for j in range(DT):
                for m in range(3):
                    t = T_O[j] + m
                    begin(t)
                    w = arrived(pe, oo + 3 * (j // 4) + m)
                    dense(t, w, (j % 4) * P, lambda k: hT[:, k, :], DT,
                          ready=("h_ready", 8 * BIASED[MIX1]) if (j, m) == (0, 0) else None)\
                        .then_inc(S["tile_done"], 1)
            for j in range(DT):
                t = T_OO + j
                begin(t)
                w = arrived(pe, oo + 6 + j // 4)
                dense(t, w, (j % 4) * P, lambda k: mixed[:, k, :], DT,
                      ready=mixed_at if j == 0 else None).then_inc(S["tile_done"], 1)
                norm_stat(FFN1, js=[j - 1] if j else [])
            norm_stat(FFN1, js=[DT - 1])
            route(1)
            experts(1)
            for m in range(8):
                tt, half = divmod(m, 2)
                turn_tile(T_OUT + m, [(xT[:, 4 * half + j, tt * P:(tt + 1) * P], P) for j in range(4)],
                          ready=(S["x_moe"], 16))

        @block.vector
        def _(dve):
            link_n = [0]

            def link(ins):
                link_n[0] += 1
                ins.then_inc(S["dve_link"], 1)
                dve.wait_ge(S["dve_link"], link_n[0])

            def scale(n, src, dst, gains, width=N):
                if n:
                    dve.wait_ge(S["scaled"], DT * n)
                dve.wait_ge(S["rms_ready"], n + 1)
                link(dve.reciprocal(rstd[:, 0:width], rms[:, 0:width]))
                for j in range(DT):
                    ins = dve.scalar_tensor_tensor(out=dst[:, j, :], in0=src[:, j, :], scalar=gains[:, j:j + 1],
                                                   in1=rstd[:, 0:width], op0=ALU.mult, op1=ALU.mult)
                    ins.then_inc(S["scaled"], 1)

            def vec(name, off=0):
                return vecT[:, COL[name] + off:COL[name] + off + 8]

            def add_to_x(t, g, j):
                dve.wait_ge(S["tile_done"], t + 1)
                dve.scalar_tensor_tensor(out=xT[:, j, :], in0=psum[:, t % 6, :], scalar=g[:, j:j + 1],
                                         in1=xT[:, j, :], op0=ALU.mult, op1=ALU.add).then_inc(FREE["dve"], 1)

            for name in ("a_ready", "y_dve", "acc_added"):
                dve.sem_inc(S[name], 1)
            for j in range(DT):
                dve.wait_ge(S["tile_done"], T_X + j + 1)
                dve.tensor_copy(xT[:, j, :], psum[:, (T_X + j) % 6, :]).then_inc(FREE["dve"], 1)
            dve.wait_ge(S["tile_done"], T_V + 1)
            for g in range(4):
                w = VEC_ROWS[g]
                ins = dve.tensor_copy(vecT[:, g * P:g * P + w], psum[:, T_V % 6, g * P:g * P + w])
                if g < 3:
                    link(ins)
            ins.then_inc(FREE["dve"], 1)
            dve.wait_ge(S["tile_done"], T_V + 2)
            dve.tensor_copy(vecT[:, 4 * P:4 * P + VEC_ROWS[4]], psum[:, (T_V + 1) % 6, 0:VEC_ROWS[4]])\
                .then_inc(FREE["dve"], 1)
            dve.wait_ge(FREE["dve"], T_V + 2)
            dve.tensor_scalar(gqk[:, 0:1], vecT[:, COL["q_g"]:COL["q_g"] + 1], HD ** -0.5, None, ALU.mult)
            dve.tensor_copy(gqk[:, 1:2], vecT[:, COL["k_g"]:COL["k_g"] + 1])
            link(dve.tensor_scalar(gqk[:, 2:3], vecT[:, COL["subln"]:COL["subln"] + 1], 1.0 - LAM_INIT, None, ALU.mult))
            dve.wait_ge(S["small_in"], 16 * 6)
            for m in range(2):
                dve.tensor_tensor_reduce(out=lam_pr[:, :], in0=lam_in[:, 2 * m, :], in1=lam_in[:, 2 * m + 1, :],
                                         scale=1.0, scalar=0.0, op0=ALU.mult, op1=ALU.add,
                                         accum_out=lam[:, m:m + 1]).then_inc(S["lam_sum"], 1)
                dve.wait_ge(S["lam_sum"], m + 1)
            dve.wait_ge(S["gains"], 1)
            scale(NORM1, xT, hT, gain[:, 0, :])

            def glu(j):
                dve.wait_ge(*emptied(T_PW1 + 2 * j)(1))
                if j == 0:
                    dve.wait_ge(S["pads_zero"], 5)
                dve.tensor_tensor(upad[:, j, :, PAD:PAD + SEG],
                                  glu_a[:, j % 2, :].rearrange("p (s w) -> p s w", s=SEGS),
                                  glu_s[:, j % 2, :].rearrange("p (s w) -> p s w", s=SEGS),
                                  ALU.mult).then_inc(S["u_ready"], 1)

            between = {(0, 0): [0], (0, 17): [1], (2, 0): [2], (2, 16): [3], (4, 0): [4], (4, 12): [5], (4, 29): [6],
                       (6, 14): [7]}
            for j in range(DT):
                if j in POOL_CONV:
                    continue
                acc = cv[:, j, :].rearrange("p (s w) -> p s w", s=SEGS)
                for k in range(TAPS):
                    for jj in between.get((j, k), ()):
                        glu(jj)
                    if k == 0:
                        dve.wait_ge(S["u_ready"], j + 1)
                    w = vecT[:, COL["w_dw"] + k * 8 + j:COL["w_dw"] + k * 8 + j + 1]
                    u = upad[:, j, :, k:k + SEG]
                    if k == 0:
                        ins = dve.tensor_scalar(acc, u, w, vecT[:, COL["b_dw"] + j:COL["b_dw"] + j + 1], ALU.mult,
                                                ALU.add)
                    else:
                        ins = dve.scalar_tensor_tensor(out=acc, in0=u, scalar=w, in1=acc, op0=ALU.mult, op1=ALU.add)
                    if k < TAPS - 1:
                        link(ins)
                ins.then_inc(S["conv_done"], 1)
            dve.wait_ge(S["conv_done"], DT - len(POOL_CONV))
            dve.wait_ge(S["tap_added"], TAPS * len(POOL_CONV))
            dve.wait_ge(S["mean_sb"], 1)
            for j in range(DT):
                dve.tensor_tensor(cv[:, j, :], cv[:, j, :], tmp[:, 0, :], ALU.subtract).then_inc(S["centered"], 1)
            dve.wait_ge(S["centered"], DT)
            scale(LN, cv, hT, vec("ln_g"))
            for j in range(DT):
                dve.wait_ge(FREE["act"], tile_free[T_PW2 + j][1])
                dve.tensor_tensor(xT[:, j, :], xT[:, j, :], tmp[:, j % 2, :], ALU.add).then_inc(S["x_pw2"], 1)
            dve.wait_ge(S["gains"], 3)
            scale(NORM2, xT, hT, gain[:, 1, :])
            for half in range(2):
                for m in range(16):
                    dve.wait_ge(FREE["act"], tile_free[T_W1[half] + m][1])
                    dve.tensor_tensor(hid[:, m, :], hid[:, m, :], hid[:, m, :], ALU.mult).then_inc(S["hid_ready"], 1)
                for j in range(DT):
                    add_to_x(T_W2[half] + j, modv[:, 0, 40:48], j)
            scale(FINAL, xT, xT, vec("final_g"))
            dve.wait_ge(S["gains"], 8)
            scale(MIX0, xT, hT, gain[:, 2, :])
            scale(CTXN, xcT, hcT, gain[:, 3, :], NC)

            dve.wait_ge(S["lam_exp"], 1)
            link(dve.tensor_tensor(lam[:, 4:5], lam[:, 3:4], lam[:, 2:3], ALU.subtract))
            link(dve.tensor_scalar(lam[:, 5:6], lam[:, 4:5], -LAM_INIT, None, ALU.add))

            def unit_norm(u):
                kind, i, t = units[u]
                w = NC if kind == "c" else N
                dve.wait_ge(S["qk_rms"], u + 1)
                link(dve.reciprocal(rstd[:, 0:w], rms[:, 0:w]))
                g = gqk[:, 0:1] if kind == "q" else gqk[:, 1:2]
                dst = kT[:, i, N:NK] if kind == "c" else qs[:, u % 4, :]
                dve.scalar_tensor_tensor(out=dst, in0=qs[:, u % 4, 0:w], scalar=g, in1=rstd[:, 0:w], op0=ALU.mult,
                                         op1=ALU.mult).then_inc(S["qk_normed"], 1)
                dve.wait_ge(S["qk_normed"], u + 1)

            rot = [0]

            def unit_done(u):
                kind, i, t = units[u]
                if kind == "c":
                    dve.nop().then_inc(S["qk_done"], 1)
                    return
                dst = qT[:, i, :] if kind == "q" else kT[:, i, 0:N]
                b = rot[0] % 2
                rot[0] += 1
                dve.tensor_tensor(t_cos[:, b, :], qs[:, u % 4, :], cos, ALU.mult)
                dve.wait_ge(S["qk_rot"], rot[0])
                link(dve.tensor_tensor(t_sin[:, b, :], psum[:, MISC, :], sin, ALU.mult))
                dve.tensor_tensor(dst, t_cos[:, b, :], t_sin[:, b, :], ALU.add).then_inc(S["qk_done"], 1)
                dve.wait_ge(S["qk_done"], u + 1)

            for u in range(len(units) + 1):
                if u < len(units):
                    unit_norm(u)
                if u >= 1:
                    unit_done(u - 1)
            for b, kind, i, t in in_tiles:
                if kind == "f":
                    dve.wait_ge(S["tile_done"], t + 1)
                    dve.tensor_copy(fT[:, i, :], psum[:, t % 6, :]).then_inc(FREE["dve"], 1)
            for t in range(NT):
                dve.wait_ge(S["tile_done"], T_F1 + t + 1)
                dve.tensor_copy(dft1[:, t, :], psum[:, (T_F1 + t) % 6, :]).then_inc(FREE["dve"], 1)
            for ft in range(2):
                dve.wait_ge(S["tile_done"], T_F2 + ft + 1)
                dve.tensor_copy(hT[:, HEADS + ft, :], psum[:, (T_F2 + ft) % 6, :]).then_inc(FREE["dve"], 1)

            def softmax_max(it):
                b = it % 2
                dve.wait_ge(S["scores"], it + 1)
                link(dve.tensor_reduce(small[:, 0:2], score_set(b), AX.X, ALU.max))
                if it >= 2:
                    dve.wait_ge(S["probs"], 2 * it - 2)
                dve.tensor_scalar(small[:, 28 + 2 * b:30 + 2 * b], small[:, 0:2], -1.0, None, ALU.mult)\
                    .then_inc(S["neg_max"], 1)
                dve.wait_ge(S["neg_max"], it + 1)

            def combine(it):
                b = it % 2
                dve.wait_ge(S["probs"], 2 * it + 2)
                link(dve.reciprocal(small[:, 8 + 4 * b:10 + 4 * b], small[:, 4 + 2 * b:6 + 2 * b]))
                link(dve.tensor_scalar(small[:, 10 + 4 * b:11 + 4 * b], small[:, 9 + 4 * b:10 + 4 * b], lam[:, 5:6],
                                       None, ALU.mult))
                if it:
                    dve.wait_ge(S["attn_ready"], it)
                w = small[:, 10 + 4 * b:11 + 4 * b]
                dve.tensor_scalar(prob1[:, N:NK], prob[:, 2 * b + 1, 0:NC], w, None, ALU.mult)
                link(dve.tensor_scalar(prob1[:, 0:N], prob[:, 2 * b + 1, NC:NK], w, None, ALU.mult))
                if it >= 2:
                    dve.wait_ge(S["attn_turned"], it - 1)
                dve.scalar_tensor_tensor(out=attn[:, b, :], in0=prob[:, 2 * b, :], scalar=small[:, 8 + 4 * b:9 + 4 * b],
                                         in1=prob1, op0=ALU.mult, op1=ALU.add)\
                    .then_inc(S["attn_ready"], 1)

            def head_norm(h):
                dve.wait_ge(S["o_rms"], h + 1)
                link(dve.reciprocal(rstd[:, :], rms[:, :]))
                dve.scalar_tensor_tensor(out=hT[:, h, :], in0=o_sb, scalar=gqk[:, 2:3], in1=rstd[:, :], op0=ALU.mult,
                                         op1=ALU.mult).then_inc(S["o_ready"], 1)
                dve.wait_ge(S["o_ready"], h + 1)

            softmax_max(0)
            for it in range(4 * HEADS):
                if it + 1 < 4 * HEADS:
                    softmax_max(it + 1)
                combine(it)
                if it > 4 and it % 4 == 1:
                    head_norm(it // 4 - 1)
            head_norm(HEADS - 1)
            for j in range(DT):
                add_to_x(T_WO + j, modv[:, 1, 16:24], j)
            scale(FFN0, xT, hT, gain[:, 4, :])

            def route_all(layer):
                lt = logits[:, :, :]

                def wide(ap):
                    return ap.unsqueeze(2).to_broadcast([P, NT, E])

                dve.wait_ge(S["tile_done"], T_LOG[layer] + 1)
                dve.tensor_copy(lgT[:, :], psum[0:E, T_LOG[layer] % 6, :]).then_inc(FREE["dve"], 1)
                t = T_LT[layer]
                dve.wait_ge(S["tile_done"], t + 1)
                ps = psum[:, t % 6, 0:NT * E].rearrange("p (a b) -> p a b", a=NT)
                link(dve.tensor_reduce(small[:, 16:20], ps, AX.X, ALU.max))
                dve.tensor_tensor(lt, ps, wide(small[:, 16:20]), ALU.subtract).then_inc(FREE["dve"], 1)
                dve.wait_ge(S["soft_exp"], layer + 1)
                link(dve.tensor_reduce(small[:, 20:24], aff[:, :, :], AX.X, ALU.add))
                link(dve.reciprocal(small[:, 24:28], small[:, 20:24]))
                dve.tensor_tensor(aff[:, :, :], aff[:, :, :], wide(small[:, 24:28]), ALU.mult)\
                    .then_inc(S["aff_ready"], 1)
                t = T_AFF[layer]
                dve.wait_ge(S["tile_done"], t + 1)
                dve.tensor_copy(left[:, :], psum[0:E, t % 6, :]).then_inc(FREE["dve"], 1)
                dve.wait_ge(*emptied(t)(0))
                for r in range(CAP // 8):
                    link(dve.max(top8[:, :], left[:, :]))
                    link(dve.match_replace(left[:, :], top8[:, :], left[:, :], -1.0))
                link(dve.tensor_scalar(affT[:, :], left[:, :], 0.0, None, ALU.is_lt))
                link(dve.tensor_tensor_scan(lgT[:, :], one[0:E, :].to_broadcast([E, N]), affT[:, :], 0.0, ALU.mult,
                                            ALU.add))
                dve.tensor_tensor(left[:, :], lgT[:, :], affT[:, :], ALU.mult).then_inc(S["pos_ready"], 1)
                t = T_POS[layer]
                dve.wait_ge(S["tile_done"], t + 1)
                dve.tensor_copy(pos[:, :, :], psum[:, t % 6, 0:NT * E].rearrange("p (a b) -> p a b", a=NT))\
                    .then_inc(FREE["dve"], 1)
                dve.wait_ge(*emptied(t)(0))
                dve.wait_ge(S["acc_zero"], layer + 1)

            def experts(layer):
                iota = const("iota").unsqueeze(1).unsqueeze(1).to_broadcast([P, NT, 2, CAP])

                def each(src, i):
                    return src[:, :, bass.ds(2 * i, 2)].unsqueeze(3).to_broadcast([P, NT, 2, CAP])

                with dve.Fori(0, PAIRS) as i:
                    n = i + PAIRS * layer
                    dve.wait_ge(S["gselT_done"], n + 1)
                    dve.tensor_tensor(sel, iota, each(pos, i), ALU.is_equal).then_inc(S["sel_ready"], 1)
                    dve.wait_ge(S["sel_ready"], n + 1)
                    dve.tensor_tensor(gsel, sel, each(aff, i), ALU.mult).then_inc(S["gsel_ready"], 1)
                    dve.wait_ge(S["gathered"], 2 * n + 2)
                    dve.tensor_copy(xsT[:, 4:8, :], psum[:, 7, :].rearrange("p (a b) -> p a b", a=4))\
                        .then_inc(S["xs_dve"], 1)
                    for half in range(2):
                        dve.wait_ge(S["up_done"], 2 * n + 2 + half)
                        dve.wait_ge(S["sil_ready"], 2 * n + 1 + half)
                        dve.tensor_tensor(act_e[:, half, :], psum[:, 2 + half, :], sil[:, half, :], ALU.mult)\
                            .then_inc(S["a_ready"], 1)
                    dve.wait_ge(S["aT_done"], 2 * n + 2)
                    dve.tensor_copy(aeT[:, 4:8, :], psum[:, 7, :].rearrange("p (a b) -> p a b", a=4))\
                        .then_inc(S["aT_dve"], 1)
                    dve.wait_ge(S["down_done"], 2 * n + 3)
                    dve.tensor_copy(y_sb[:, N:D], psum[:, 5, :]).then_inc(S["y_dve"], 1)
                    for fj in range(DT):
                        dve.wait_ge(S["scattered"], 8 * n + fj + 1)
                        dve.tensor_tensor(hT[:, fj, :], hT[:, fj, :], psum[:, 6 + fj % 2, :], ALU.add)\
                            .then_inc(S["acc_added"], 1)
                v = 1 if layer == 0 else 3
                dve.wait_ge(S["acc_added"], 8 * PAIRS * (layer + 1) + 1)
                for j in range(DT):
                    dve.scalar_tensor_tensor(out=xT[:, j, :], in0=hT[:, j, :], scalar=modv[:, v, 40 + j:41 + j],
                                             in1=xT[:, j, :], op0=ALU.mult, op1=ALU.add).then_inc(S["x_moe"], 1)
                dve.wait_ge(S["x_moe"], 8 * layer + 8)

            route_all(0)
            experts(0)
            scale(MIX1, xT, hT, gain[:, 5, :])
            dve.memset(zpad[:, 0:1], 0.0)
            link(dve.memset(zpad[:, N + 1:N + 2], 0.0))
            for j in range(DT):
                t = T_O[j]
                dve.wait_ge(S["tile_done"], t + 2)
                dve.wait_ge(FREE["act"], tile_free[t][1])
                dve.tensor_tensor(zpad[:, 1:N + 1], psum[:, (t + 1) % 6, :], cg[:, j % 2, :], ALU.mult)\
                    .then_inc(FREE["dve"], 1)
                dve.wait_ge(FREE["dve"], tile_free[t + 1][1])
                for k in range(3):
                    w = vecT[:, COL["w_conv3"] + 8 * k + j:COL["w_conv3"] + 8 * k + j + 1]
                    if k == 0:
                        link(dve.tensor_scalar(zc, zpad[:, 0:N], w, None, ALU.mult))
                    else:
                        link(dve.scalar_tensor_tensor(out=zc, in0=zpad[:, k:k + N], scalar=w, in1=zc, op0=ALU.mult,
                                                      op1=ALU.add))
                dve.wait_ge(S["tile_done"], t + 3)
                dve.tensor_tensor(mixed[:, j, :], psum[:, (t + 2) % 6, :], zc, ALU.mult).then_inc(FREE["dve"], 1)
            for j in range(DT):
                add_to_x(T_OO + j, modv[:, 3, 16:24], j)
            scale(FFN1, xT, hT, gain[:, 6, :])
            route_all(1)
            experts(1)
            for m in range(8):
                tt, half = divmod(m, 2)
                t = T_OUT + m
                dve.wait_ge(S["tile_done"], t + 1)
                dve.tensor_copy(out_tok[:, tt, half * N:(half + 1) * N], psum[:, t % 6, :]).then_inc(FREE["dve"], 1)


_INS = ["x", "c", "w_mod", "b_mod", "norm1_g", "norm2_g", "final_g", "conv_w_pw1", "conv_b_pw1", "conv_w_dw",
        "conv_b_dw", "conv_ln_g", "conv_ln_b", "conv_w_pw2", "conv_b_pw2", "mlp_w1", "mlp_w2", "c_2", "ctx_2",
        "c_ctx_2", "ada_w_2", "ada_b_2", "norm_mix_2", "norm_ffn_2", "attn_w_in_2", "attn_q_norm_2",
        "attn_k_norm_2", "lam_q1_2", "lam_k1_2", "lam_q2_2", "lam_k2_2", "attn_subln_2", "attn_w_out_2",
        "conv_w_in_2", "conv_w_2", "conv_w_out_2", "router_w_2", "moe_w_gate_2", "moe_w_up_2", "moe_w_down_2"]


def kernel(**inputs):
    import concourse.bacc as _bacc
    from concourse.bass_utils import run_bass_kernel_spmd as _run

    nc = _bacc.Bacc("TRN2", target_bir_lowering=False, num_devices=1)
    const_k, dft_n = constants()
    given = {name: np.ascontiguousarray(inputs[name]) for name in _INS}
    given["const_k"], given["dft_n"] = const_k, dft_n
    arrays, aps = {}, {}
    for name, a in given.items():
        arrays[f"in_{name}_dram"] = a
        aps[name] = nc.dram_tensor(f"in_{name}_dram", a.shape, mybir.dt.from_np(a.dtype), kind="ExternalInput").ap()
    out = nc.dram_tensor("out_0_dram", (1, N, D), F32, kind="ExternalOutput").ap()
    block_kernel(nc, aps, out)
    r = _run(nc, [arrays], core_ids=[0])
    return r.results[0]["out_0_dram"]
```
